# Optimizing a Trainium2 kernel written in Bass

```python
import jax, jax.numpy as jnp
from jax import lax
import numpy as np

D_MODEL = 2048
BATCH = 1
SEQ = 256
DEPTH = 1

CTX_LEN = 256
GRID_W = 64
D_MIX = D_MODEL
D_LRU = D_MIX // 2
LRU_BLOCKS = 8
LRU_BS = D_LRU // LRU_BLOCKS
CONV_W = 4
LRU_C = 8.0
D_MV = D_MIX - D_LRU
M_HEADS = 8
M_DV = D_MV // M_HEADS
M_DK = M_DV // 2
D_MQK = M_HEADS * M_DK
CHUNK = 128
D_FF = ((8 * D_MODEL // 3 + 255) // 256) * 256
N_MOD = 9
EPS = 1e-6
HALF = 0.5
IN_WIDTHS = (D_LRU, D_LRU, D_MQK, D_MQK, D_MV, D_MV, 4 * M_HEADS)
D_IN = sum(IN_WIDTHS)
SPLITS = [int(s) for s in np.cumsum(IN_WIDTHS)[:-1]]

kernel_name = "hybrid_rglru_mlstm_macaron_dit_block"

def rmsnorm(x, g):
    xf = x.astype(jnp.float32)
    y = xf * lax.rsqrt(jnp.mean(xf * xf, axis=-1, keepdims=True) + EPS)
    return (y * g.astype(jnp.float32)).astype(x.dtype)

def modulate(h, shift, scale):
    return h * (1 + scale) + shift

def swiglu(h, w_up, w_down):
    gate, up = jnp.split(h @ w_up, 2, axis=-1)
    return (jax.nn.silu(gate) * up) @ w_down

def centred_conv(x, w, b):
    T = x.shape[1]
    lo = CONV_W // 2
    xp = jnp.pad(x, ((0, 0), (lo, CONV_W - 1 - lo), (0, 0)))
    return b + sum(xp[:, k:k + T] * w[k] for k in range(CONV_W))

def linear_scan(a, bx, h0):
    bx = bx.at[:, 0].add(a[:, 0] * h0)

    def combine(l, r):
        al, bl = l
        ar, br = r
        return al * ar, ar * bl + br

    _, h = lax.associative_scan(combine, (a, bx), axis=1)
    return h

def rglru_dir(xc, w_r, b_r, w_i, b_i, lam, h0):
    B, T, _ = xc.shape
    xb = xc.reshape(B, T, LRU_BLOCKS, LRU_BS)
    r = jax.nn.sigmoid(jnp.einsum('btnc,ncd->btnd', xb, w_r).reshape(B, T, D_LRU) + b_r)
    i = jax.nn.sigmoid(jnp.einsum('btnc,ncd->btnd', xb, w_i).reshape(B, T, D_LRU) + b_i)
    log_a = -LRU_C * r * jax.nn.softplus(-lam.astype(jnp.float32))
    a = jnp.exp(log_a)
    mult = jnp.sqrt(-jnp.expm1(2.0 * log_a))
    return linear_scan(a, mult * i * xc, h0)

def rglru_bidir(u_lat, u_ctx, conv_w, conv_b, w_r, b_r, w_i, b_i, lam):
    f32 = jnp.float32
    xl = centred_conv(u_lat.astype(f32), conv_w, conv_b)
    xc = centred_conv(u_ctx.astype(f32), conv_w, conv_b)
    z = jnp.zeros((xc.shape[0], D_LRU), f32)

    def run(d, seq, h0):
        return rglru_dir(seq, w_r[d], b_r[d], w_i[d], b_i[d], lam[d], h0)

    hc_f = run(0, xc, z)
    hl_f = run(0, xl, hc_f[:, -1])
    hc_b = run(1, xc[:, ::-1], z)
    hl_b = run(1, xl[:, ::-1], hc_b[:, -1])
    return hl_f + hl_b[:, ::-1], hc_f + hc_b[:, ::-1]

def mlstm_dir(q, k, v, ig, fg, state0):
    B, H, T, DK = q.shape
    DV = v.shape[-1]
    nc = T // CHUNK

    def chunks(t):
        t = t.reshape((B, H, nc, CHUNK) + t.shape[3:])
        return jnp.moveaxis(t, 2, 0)

    log_f = jax.nn.log_sigmoid(fg)
    lower = jnp.tril(jnp.ones((CHUNK, CHUNK), dtype=bool))

    def step(state, xs):
        C, n, m = state
        qc, kc, vc, ic, lfc = xs
        bcum = jnp.cumsum(lfc, axis=-1)
        dmat = bcum[..., :, None] - bcum[..., None, :] + ic[..., None, :]
        dmat = jnp.where(lower, dmat, -jnp.inf)
        inter = bcum + m[..., None]
        m_row = jnp.maximum(inter, jnp.max(dmat, axis=-1))
        w = jnp.einsum('bhtk,bhsk->bhts', qc, kc) * jnp.exp(dmat - m_row[..., None])
        s_inter = jnp.exp(inter - m_row)
        num = s_inter[..., None] * jnp.einsum('bhvk,bhtk->bhtv', C, qc) + jnp.einsum('bhts,bhsv->bhtv', w, vc)
        den = s_inter * jnp.einsum('bhk,bhtk->bht', n, qc) + jnp.sum(w, axis=-1)
        h = num / jnp.maximum(jnp.abs(den), jnp.exp(-m_row))[..., None]
        b_last = bcum[..., -1]
        g = b_last[..., None] - bcum + ic
        m_new = jnp.maximum(b_last + m, jnp.max(g, axis=-1))
        decay = jnp.exp(b_last + m - m_new)
        wg = jnp.exp(g - m_new[..., None])
        C_new = decay[..., None, None] * C + jnp.einsum('bhs,bhsv,bhsk->bhvk', wg, vc, kc)
        n_new = decay[..., None] * n + jnp.einsum('bhs,bhsk->bhk', wg, kc)
        return (C_new, n_new, m_new), h

    state, hs = lax.scan(step, state0, (chunks(q), chunks(k), chunks(v), chunks(ig), chunks(log_f)))
    h = jnp.moveaxis(hs, 0, 2).reshape(B, H, T, DV)
    return h, state

def mlstm_prep(q, k, v, gt):
    f32 = jnp.float32
    B, T, _ = q.shape

    def heads(t, d):
        return t.astype(f32).reshape(B, T, M_HEADS, d).transpose(0, 2, 1, 3)

    gates = gt.astype(f32).reshape(B, T, 4, M_HEADS).transpose(2, 0, 3, 1)
    return heads(q, M_DK), heads(k, M_DK) * (M_DK ** -0.5), heads(v, M_DV), gates

def mlstm_bidir(lat, ctx_in):
    ql, kl, vl, gl = lat
    qc, kc, vc, gc = ctx_in
    B = qc.shape[0]
    f32 = jnp.float32
    zero = (jnp.zeros((B, M_HEADS, M_DV, M_DK), f32), jnp.zeros((B, M_HEADS, M_DK), f32),
            jnp.zeros((B, M_HEADS), f32))

    def fl(t):
        return jnp.flip(t, axis=2)

    hc_f, st_f = mlstm_dir(qc, kc, vc, gc[0], gc[1], zero)
    hl_f, _ = mlstm_dir(ql, kl, vl, gl[0], gl[1], st_f)
    hc_b, st_b = mlstm_dir(fl(qc), fl(kc), fl(vc), jnp.flip(gc[2], -1), jnp.flip(gc[3], -1), zero)
    hl_b, _ = mlstm_dir(fl(ql), fl(kl), fl(vl), jnp.flip(gl[2], -1), jnp.flip(gl[3], -1), st_b)
    return hl_f + fl(hl_b), hc_f + fl(hc_b)

def mlstm_headnorm(hh, gain):
    B, H, T, DV = hh.shape
    hh = hh * lax.rsqrt(jnp.mean(hh * hh, axis=-1, keepdims=True) + EPS)
    return hh.transpose(0, 2, 1, 3).reshape(B, T, H * DV) * gain.astype(jnp.float32)

def to_colmajor(t, rows):
    B, T, F = t.shape
    return t.reshape(B, rows, GRID_W, F).transpose(0, 2, 1, 3).reshape(B, T, F)

def from_colmajor(t, rows):
    B, T, F = t.shape
    return t.reshape(B, GRID_W, rows, F).transpose(0, 2, 1, 3).reshape(B, T, F)

def token_mix(h, hc, rows, is_last, w_in, b_mgate, lru_conv_w, lru_conv_b, lru_w_r, lru_b_r,
              lru_w_i, lru_b_i, lru_lam, mlstm_norm, w_out):
    lx, lg, q, k, v, o, gt = jnp.split(h @ w_in, SPLITS, axis=-1)
    lxc, lgc, qc, kc, vc, oc, gtc = jnp.split(hc @ w_in, SPLITS, axis=-1)
    f32 = jnp.float32
    rl, rc = rglru_bidir(lx, lxc, lru_conv_w, lru_conv_b, lru_w_r, lru_b_r, lru_w_i, lru_b_i, lru_lam)
    lru_lat = jax.nn.gelu(lg.astype(f32)) * rl
    cm = lambda t: to_colmajor(t, rows)
    ml, mc = mlstm_bidir(mlstm_prep(cm(q), cm(k), cm(v), cm(gt) + b_mgate),
                         mlstm_prep(qc, kc, vc, gtc + b_mgate))
    mls_lat = from_colmajor(mlstm_headnorm(ml, mlstm_norm), rows) * jax.nn.sigmoid(o.astype(f32))
    y = jnp.concatenate([lru_lat, mls_lat], axis=-1).astype(h.dtype) @ w_out
    if is_last:
        return y, None
    lru_c = jax.nn.gelu(lgc.astype(f32)) * rc
    mls_c = mlstm_headnorm(mc, mlstm_norm) * jax.nn.sigmoid(oc.astype(f32))
    yc = jnp.concatenate([lru_c, mls_c], axis=-1).astype(hc.dtype) @ w_out
    return y, yc

def layer(x, ctx, mod, mod_c, rows, is_last, ffn1_norm, ffn1_w_up, ffn1_w_down, mix_norm, w_in,
          b_mgate, lru_conv_w, lru_conv_b, lru_w_r, lru_b_r, lru_w_i, lru_b_i, lru_lam, mlstm_norm,
          w_out, ffn2_norm, ffn2_w_up, ffn2_w_down):
    sh1, sc1, g1, sh2, sc2, g2, sh3, sc3, g3 = jnp.split(mod, N_MOD, axis=-1)
    csh1, csc1, cg1, csh2, csc2, cg2, csh3, csc3, cg3 = jnp.split(mod_c, N_MOD, axis=-1)
    x = x + HALF * g1 * swiglu(modulate(rmsnorm(x, ffn1_norm), sh1, sc1), ffn1_w_up, ffn1_w_down)
    ctx = ctx + HALF * cg1 * swiglu(modulate(rmsnorm(ctx, ffn1_norm), csh1, csc1), ffn1_w_up, ffn1_w_down)
    h = modulate(rmsnorm(x, mix_norm), sh2, sc2)
    hc = modulate(rmsnorm(ctx, mix_norm), csh2, csc2)
    y, yc = token_mix(h, hc, rows, is_last, w_in, b_mgate, lru_conv_w, lru_conv_b, lru_w_r, lru_b_r,
                      lru_w_i, lru_b_i, lru_lam, mlstm_norm, w_out)
    x = x + g2 * y
    x = x + HALF * g3 * swiglu(modulate(rmsnorm(x, ffn2_norm), sh3, sc3), ffn2_w_up, ffn2_w_down)
    if not is_last:
        ctx = ctx + cg2 * yc
        ctx = ctx + HALF * cg3 * swiglu(modulate(rmsnorm(ctx, ffn2_norm), csh3, csc3), ffn2_w_up, ffn2_w_down)
    return x, ctx

def setup_inputs(seed: int = 0) -> dict:
    key = jax.random.key(seed)
    ks = jax.random.split(key, 32)
    f32 = jnp.float32

    def nrm(k, shape, s):
        return jax.random.normal(k, shape, f32) * s

    x = nrm(ks[0], (BATCH, SEQ, D_MODEL), 1.0)
    c = nrm(ks[1], (BATCH, D_MODEL), 1.0)
    ctx = nrm(ks[2], (BATCH, CTX_LEN, D_MODEL), 1.0)
    c_ctx = nrm(ks[3], (D_MODEL,), 1.0)
    ada_w = nrm(ks[4], (DEPTH, D_MODEL, N_MOD * D_MODEL), 0.5 * D_MODEL ** -0.5)
    ada_b = nrm(ks[5], (DEPTH, N_MOD * D_MODEL), 0.01)
    ffn1_norm = 1.0 + nrm(ks[6], (DEPTH, D_MODEL), 0.01)
    ffn1_w_up = nrm(ks[7], (DEPTH, D_MODEL, 2 * D_FF), D_MODEL ** -0.5)
    ffn1_w_down = nrm(ks[8], (DEPTH, D_FF, D_MODEL), D_FF ** -0.5)
    mix_norm = 1.0 + nrm(ks[9], (DEPTH, D_MODEL), 0.01)
    w_in = nrm(ks[10], (DEPTH, D_MODEL, D_IN), D_MODEL ** -0.5)
    f_off = jnp.stack([jnp.zeros((M_HEADS,), f32), jnp.linspace(3.0, 6.0, M_HEADS, dtype=f32)])
    b_mgate = (nrm(ks[11], (DEPTH, 2, 2, M_HEADS), 0.1) + f_off).reshape(DEPTH, 4 * M_HEADS)
    lru_conv_w = nrm(ks[12], (DEPTH, CONV_W, D_LRU), CONV_W ** -0.5)
    lru_conv_b = nrm(ks[13], (DEPTH, D_LRU), 0.01)
    lru_w_r = nrm(ks[14], (DEPTH, 2, LRU_BLOCKS, LRU_BS, LRU_BS), LRU_BS ** -0.5)
    lru_b_r = nrm(ks[15], (DEPTH, 2, D_LRU), 0.01)
    lru_w_i = nrm(ks[16], (DEPTH, 2, LRU_BLOCKS, LRU_BS, LRU_BS), LRU_BS ** -0.5)
    lru_b_i = nrm(ks[17], (DEPTH, 2, D_LRU), 0.01)
    a0 = jax.random.uniform(ks[18], (DEPTH, 2, D_LRU), f32, minval=0.9, maxval=0.999)
    lru_lam = jnp.log(a0) - jnp.log1p(-a0)
    mlstm_norm = 1.0 + nrm(ks[19], (DEPTH, D_MV), 0.01)
    w_out = nrm(ks[20], (DEPTH, D_MIX, D_MODEL), D_MIX ** -0.5)
    ffn2_norm = 1.0 + nrm(ks[21], (DEPTH, D_MODEL), 0.01)
    ffn2_w_up = nrm(ks[22], (DEPTH, D_MODEL, 2 * D_FF), D_MODEL ** -0.5)
    ffn2_w_down = nrm(ks[23], (DEPTH, D_FF, D_MODEL), D_FF ** -0.5)
    final_norm = 1.0 + nrm(ks[24], (D_MODEL,), 0.01)
    return {"x": x, "c": c, "ctx": ctx, "c_ctx": c_ctx, "ada_w": ada_w, "ada_b": ada_b,
            "ffn1_norm": ffn1_norm, "ffn1_w_up": ffn1_w_up, "ffn1_w_down": ffn1_w_down,
            "mix_norm": mix_norm, "w_in": w_in, "b_mgate": b_mgate, "lru_conv_w": lru_conv_w,
            "lru_conv_b": lru_conv_b, "lru_w_r": lru_w_r, "lru_b_r": lru_b_r, "lru_w_i": lru_w_i,
            "lru_b_i": lru_b_i, "lru_lam": lru_lam, "mlstm_norm": mlstm_norm, "w_out": w_out,
            "ffn2_norm": ffn2_norm, "ffn2_w_up": ffn2_w_up, "ffn2_w_down": ffn2_w_down,
            "final_norm": final_norm}

def reference(x, c, ctx, c_ctx, ada_w, ada_b, ffn1_norm, ffn1_w_up, ffn1_w_down, mix_norm, w_in,
              b_mgate, lru_conv_w, lru_conv_b, lru_w_r, lru_b_r, lru_w_i, lru_b_i, lru_lam,
              mlstm_norm, w_out, ffn2_norm, ffn2_w_up, ffn2_w_down, final_norm):
    rows = x.shape[1] // GRID_W
    sc = jax.nn.silu(c)
    sc_ctx = jax.nn.silu(c_ctx)
    for l in range(DEPTH):
        mod = (sc @ ada_w[l] + ada_b[l])[:, None, :]
        mod_c = (sc_ctx @ ada_w[l] + ada_b[l])[None, None, :]
        x, ctx = layer(x, ctx, mod, mod_c, rows, l == DEPTH - 1, ffn1_norm[l], ffn1_w_up[l],
                       ffn1_w_down[l], mix_norm[l], w_in[l], b_mgate[l], lru_conv_w[l], lru_conv_b[l],
                       lru_w_r[l], lru_b_r[l], lru_w_i[l], lru_b_i[l], lru_lam[l], mlstm_norm[l],
                       w_out[l], ffn2_norm[l], ffn2_w_up[l], ffn2_w_down[l])
    return rmsnorm(x, final_norm)


_drawn_inputs = setup_inputs


def setup_inputs(seed=0):
    import zlib

    import numpy as np

    out = dict(_drawn_inputs(seed))
    spreads = {}
    factors = {'ada_b': 3.685,
     'ffn1_norm': 8.0,
     'mix_norm': 22.177,
     'lru_conv_b': 23.34,
     'lru_b_r': 54.647,
     'lru_b_i': 49.392,
     'mlstm_norm': 200.0,
     'ffn2_norm': 200.0,
     'final_norm': 190.48}
    for name, (base, spread) in spreads.items():
        noise = np.random.default_rng([zlib.crc32(name.encode()), seed]).standard_normal(out[name].shape)
        drawn = base * np.exp(spread * noise) if base else spread * noise
        out[name] = __import__('jax').numpy.asarray(drawn.astype(out[name].dtype))
    for name, factor in factors.items():
        out[name] = (out[name] * factor).astype(out[name].dtype)
    return out
```

```python
import concourse.bass as bass
from concourse import mybir
from contextlib import ExitStack

P = 128
D_MODEL, D_FF, N_MOD = 2048, 5632, 9
SEQ = CTX = 256
GRID_W = 64
ROWS = SEQ // GRID_W
DT = D_MODEL // P
HEADS, DK, DV = 8, 64, 128
LRU_N = 8
EPS = 1e-6
LX0, LG0, Q0, K0, V0, O0, GT0 = 0, 1024, 2048, 2560, 3072, 4096, 5120
GROUPS = D_FF // 512
UW = 2048
VS = 129

LATE = [(0, 3), (0, 4), (1, 3), (1, 4), (1, 5), (1, 6), (1, 7), (1, 8)]
_COLS = [("ada_b", N_MOD * DT), ("ada_bx", (len(LATE) + 1) * DT), ("n1", DT), ("n2", DT), ("n3", DT), ("nf", DT), ("conv_w", 32), ("conv_b", 8),
         ("b_r", 16), ("b_i", 16), ("lam", 16), ("c", 2 * DT), ("mg", 2), ("mnorm", 8)]
_CONST = [("ident", P), ("maskf", P), ("maskb", P), ("ones", P), ("parity", P), ("jj", 32), ("sel", 80), ("comb", 2),
          ("one", 1), ("eps", 1)]


def _offsets(cols):
    at, out = 0, {}
    for name, n in cols:
        out[name] = (at, at + n)
        at += n
    return out, at


VEC, NVEC = _offsets(_COLS)
CST, NCST = _offsets(_CONST)


def hybrid_layer(nc, xT, vec, cst, lru_w, ada_w, w_up1, w_dn1, w_in, w_out, w_up2, w_dn2, out):
    F, R = mybir.dt.float32, mybir.dt.float32r
    ACT, ALU, AX = mybir.ActivationFunctionType, mybir.AluOpType, mybir.AxisListType

    ADA0 = 0
    FF1 = ADA0 + 3 * DT
    MIX = FF1 + 12 * GROUPS
    MIX_UNITS = ([("gt", 0, 0)] + [("lx", p, h) for p in range(4) for h in range(2)]
                 + [("k", p, h) for p in range(2) for h in range(2)] + [("v", p, h) for p in range(4) for h in range(2)]
                 + [("q", p, h) for p in range(2) for h in range(2)] + [("lg", p, h) for p in range(4) for h in range(2)]
                 + [("o", p, h) for p in range(2) for h in range(4)]
                 + [("woa", p, 0) for p in range(8)] + [("wob", p, 0) for p in range(8)])
    FF2 = MIX + len(MIX_UNITS)
    UNITS = FF2 + 12 * GROUPS
    TICK = {u: i for i, u in enumerate(MIX_UNITS)}

    ctx = ExitStack()
    with ctx:
        def sb(name, shape, dt=F, scope=ctx):
            return scope.enter_context(nc.sbuf_tensor(name, shape, dt))

        V = sb("vectors", [P, NVEC])
        K = sb("constants", [P, NCST])
        mod = sb("mod", [P, 2, 3, DT])
        modx = sb("mod_late", [P, 9, DT])
        scl = sb("norm_scale", [P, 3, 2, DT])
        hgate = sb("half_gate", [P, 2, 2, DT])
        silc = sb("silu_c", [P, 2 * DT])
        CH = sb("cond_hi", [P, DT, 4], R)
        CL = sb("cond_hi_only", [P, DT, 4], R)
        X = sb("residual", [P, 2, DT, SEQ])
        stage = sb("stage", [P, 3, UW])
        WH = sb("w_hi", [P, 2, UW], R)
        WL = sb("w_lo", [P, 2, UW], R)
        lsp = sb("lru_rate", [P, 2, 16])
        rate = sb("rate_work", [P, 3, 16])
        zer = sb("zeros", [P, P])

        with ExitStack() as s1:
            XHL = sb("x_hi_lo", [P, 2, 2, DT, SEQ], R, s1)
            with ExitStack() as s2:
                HHL = sb("hidden_hi_lo", [P, 2, 4, 512], R, s2)
                G = sb("gate_act", [P, 2, 512], F, s2)
                U = sb("up_sum", [P, 2, 512], F, s2)
                with ExitStack() as s3:
                    sq = sb("squares", [P, 2, 512], F, s3)
                    rms = sb("rms", [P, 512], F, s3)
                    xn = sb("normed", [P, 2, 512], F, s3)
                    xm = sb("modulated", [P, 2, 512], F, s3)
                    rows4 = sb("ada_rows", [4, UW], F, s3)
                with ExitStack() as s3:
                    acc = sb("ada_sums", [P, UW], F, s3)
                    astage = sb("ada_stage", [P, 2, UW], F, s3)
            with ExitStack() as s2:
                mixA = sb("mixer_pool", [P, 32 * VS + 3 * 2048 + 516 + 512 + 400 + 32 + 68], F, s2)
                with ExitStack() as s3:
                    xpad = sb("conv_in", [P, LRU_N, 2, 260], F, s3)
                with ExitStack() as s3:
                    MXA = sb("mix_lru_hi_lo", [P, 2, 8, SEQ], R, s3)
        with ExitStack() as s1:
            scr = sb("mixer_scratch", [P, 8192], F, s1)
            MXB = sb("mix_mlstm_hi_lo", [P, 2, 8, SEQ], R, s1)
        with ExitStack() as s1:
            XL2 = sb("x2_hi_lo", [P, 2, DT, SEQ], R, s1)

        def carve(pool, sizes):
            at, out = 0, []
            for n in sizes:
                out.append(pool[:, at:at + n])
                at += n
            return out

        vaug, knat, LO, rows, LW, kw, tr, dec, mst = carve(
            mixA, [4 * 8 * VS, 4 * 512, 8 * 256, 4 * 512, 516, 512, 400, 32, 68])
        vaug = vaug.rearrange("p (c h v) -> p c h v", c=4, h=8)
        knat = knat.rearrange("p (c n) -> p c n", c=4)
        LO = LO.rearrange("p (b t) -> p b t", b=8)
        rows = rows.rearrange("p (q t) -> p q t", q=4)
        t1 = LW[:, 0:4 * 129].rearrange("p (h v) -> p h v", h=4)
        LW = LW[:, 0:512].rearrange("p (g n) -> p g n", g=4)
        tr = tr.rearrange("p (q n) -> p q n", q=10)
        kT, qz, C, Hs, Dx = carve(scr, [4 * 256, 2 * 4 * 256, 2 * 4 * 258, 2 * 8 * P, 512])
        kT = kT.rearrange("p (j t) -> p j t", j=4)
        qz = qz.rearrange("p (a j t) -> p a j t", a=2, j=4)
        C = C.rearrange("p (d j n) -> p d j n", d=2, j=4)
        Hs = Hs.rearrange("p (c h v) -> p c h v", c=2, h=8)
        Dx = Dx.rearrange("p (h t) -> p h t", h=4)
        late = X[:, 0, :, :].rearrange("p k t -> p (k t)")
        Rg, Ig, Ag, xc = carve(late, [1024, 1024, 1024, 1024])
        Rg = Rg.rearrange("p (d t) -> p d t", d=2)
        Ig = Ig.rearrange("p (d t) -> p d t", d=2)
        Ag = Ag.rearrange("p (d t) -> p d t", d=2)
        xc = xc.rearrange("p (a t) -> p a t", a=2)
        GT = xc[0:32, 0, :]
        lgs, SO = carve(late, [2048, 2048])
        lgs = lgs.rearrange("p (b t) -> p b t", b=8)
        SO = SO.rearrange("p (c n) -> p c n", c=2)

        ps = ctx.enter_context(nc.psum_tensor("psum", [P, 8, 512], F))

        def v_(name, a=0, b=None):
            lo, hi = VEC[name]
            return V[:, lo + a:(hi if b is None else lo + b)]

        def c_(name, a=0, b=None):
            lo, hi = CST[name]
            return K[:, lo + a:(hi if b is None else lo + b)]

        def sem(name):
            return ctx.enter_context(nc.semaphore(name))

        params_in, x_in, lruw_in, out_ready, out_done = (sem(n) for n in (
            "params_in", "x_in", "lruw_in", "out_ready", "out_done"))
        stage_full = [sem(f"stage_full{i}") for i in range(3)]
        hi_done, lo_done, unit_used = sem("hi_done"), sem("lo_done"), sem("unit_used")
        half_free = [sem("psum_lo_free"), sem("psum_hi_free")]
        zeros_set, cond_silu, cond_ready = sem("zeros_set"), sem("cond_silu"), sem("cond_ready")
        col_done, sq_done, sq_used, var_ready, root_ready, rms_ready = (sem(n) for n in (
            "col_done", "sq_done", "sq_used", "var_ready", "root_ready", "rms_ready"))
        xn_done, xm_done, xsplit = sem("xn_done"), sem("xm_done"), sem("x_split")
        gate_lo, gate_sum, silu_done, up_lo, prod_done, hid_hi, hid_ready = (sem(n) for n in (
            "gate_lo", "gate_sum", "silu_done", "up_lo", "prod_done", "hid_hi", "hid_ready"))
        dve_step, act_step, add_first = sem("dve_step"), sem("act_step"), sem("add_first")
        log_done, enm_arg, exp_rows, dec_rhs = (sem(n) for n in (
            "log_done", "enm_arg", "exp_rows", "dec_rhs"))
        conv_first, conv_done, act_a, z_done, root_z, lru_done = (sem(n) for n in (
            "conv_first", "conv_done", "lru_act_a", "lru_z", "lru_root", "lru_done"))
        rate_arg, rate_exp, rate_u, rate_ln = sem("rate_arg"), sem("rate_exp"), sem("rate_u"), sem("rate_ln")
        qz_zero, lo_copy, kw_done = (sem(n) for n in (
            "qz_zero", "lo_copy", "kw_done"))
        d_masked, d_exp, inter_done, num_done = (sem(n) for n in (
            "d_masked", "d_exp", "inter_done", "num_done"))
        gelu_done, lru_mul, mxa_hi, mxa_done = (sem(n) for n in (
            "gelu_done", "lru_mul", "mxa_hi", "mxa_done"))
        hms, hroot, hn_done, mxb_hi, mxb_done = (sem(n) for n in (
            "head_ms", "head_root", "head_normed", "mxb_hi", "mxb_done"))
        pads_set = sem("pads_set")
        ada_full = [sem("ada_full0"), sem("ada_full1")]
        sums_done, late_cols, late_read = sem("ada_sums_done"), sem("late_cols"), sem("late_read")
        bulk_free = [sem("bulk0_free"), sem("bulk1_free")]
        ext_done, ext_free = sem("ext_done"), sem("ext_free")
        block = ctx.enter_context(nc.Block())

        H_FF1 = 3
        H_FF2 = H_FF1 + 3 * GROUPS

        ADA_TICKS = {1: (0, 1), 2: (2, 3, 4), 4: (5, 6, 7), 5: (8, 9), 6: (10, 11, 12), 8: (13,), 9: (14,), 10: (15,)}
        assert [k for t in sorted(ADA_TICKS) for k in ADA_TICKS[t]] == list(range(DT))

        def unit_src(i):
            kind, p, h = MIX_UNITS[i]
            if kind == "gt":
                return w_in[:, GT0:GT0 + 32].rearrange("(k p) c -> p k c", p=P), 16, 32
            if kind == "o":
                return w_in[h * 512:(h + 1) * 512, O0 + p * 512:O0 + (p + 1) * 512].rearrange(
                    "(k p) c -> p k c", p=P), 4, 512
            if kind in ("woa", "wob"):
                r = 1024 * (kind == "wob")
                return w_out[r:r + 1024, p * 256:(p + 1) * 256].rearrange("(k p) c -> p k c", p=P), 8, 256
            c = {"lx": LX0, "k": K0, "v": V0, "q": Q0, "lg": LG0}[kind] + p * 256
            return w_in[h * 1024:(h + 1) * 1024, c:c + 256].rearrange("(k p) c -> p k c", p=P), 8, 256

        def wv(w, slot, k, c):
            return w[:, slot, 0:k * c].rearrange("p (k c) -> p k c", k=k)

        @block.sync
        def _(sp):
            sp.dma_start(V[:], vec).then_inc(params_in, 16)
            sp.dma_start(K[:], cst).then_inc(params_in, 16)

            def load(n, slot, k, c, src, at):
                if n >= 3:
                    sp.wait_ge(lo_done, at - 2)
                sp.dma_start(wv(stage, slot, k, c), src).then_inc(stage_full[slot], 16)

            for b in range(3):
                for k in range(DT):
                    n = b * DT + k
                    load(n, n % 3, 1, UW, ada_w[k * P:(k + 1) * P, b * UW:(b + 1) * UW].rearrange(
                        "(k p) c -> p k c", p=P), n)
                    if n == 2:
                        for s in range(2):
                            sp.dma_start(X[:, s], xT[:, s * DT:(s + 1) * DT, :]).then_inc(x_in, 16)

            def ffn_loads(base, w_up, w_dn, g, g_at, block=None):
                for u in range(12):
                    if block is not None and u >= 2:
                        ada_loads(g, block, (9, 10) if u == 11 else (u - 2,))
                    n = base + u
                    if u < 8:
                        half, up, kh = u // 4, (u // 2) % 2, u % 2
                        c = up * D_FF + half * 256
                        src = w_up[kh * 1024:(kh + 1) * 1024, bass.ds(g * 512 + c, 256)].rearrange(
                            "(k p) c -> p k c", p=P)
                        load(n, n % 3, 8, 256, src, n + g_at)
                    else:
                        src = w_dn[bass.ds(g * 512, 512), (u - 8) * 512:(u - 7) * 512].rearrange(
                            "(k p) c -> p k c", p=P)
                        load(n, n % 3, 4, 512, src, n + g_at)

            def ada_loads(g, block, ticks):
                for t in ticks:
                    if t == 1:
                        sp.wait_ge(col_done, 3)
                        sp.wait_ge(xsplit, DT)
                    for k in ADA_TICKS.get(t, ()):
                        sp.wait_ge(sums_done, 16 * g + k + 1)
                        sp.dma_start(astage[:, k % 2, :], ada_w[k * P:(k + 1) * P, bass.ds(block * UW, UW)]).then_inc(
                            ada_full[k % 2], 16)

            with nc.sync.Fori(0, 2) as g:
                ffn_loads(FF1, w_up1, w_dn1, g, 12 * g, g + 3)
            with nc.sync.Fori(2, 8) as g:
                ffn_loads(FF1, w_up1, w_dn1, g, 12 * g, g + 1)
            with nc.sync.Fori(8, GROUPS) as g:
                ffn_loads(FF1, w_up1, w_dn1, g, 12 * g)
            for i in range(len(MIX_UNITS)):
                src, k, c = unit_src(i)
                load(MIX + i, (MIX + i) % 3, k, c, src, MIX + i)
            with nc.sync.Fori(0, GROUPS) as g:
                ffn_loads(FF2, w_up2, w_dn2, g, 12 * g)
            for q in range(4):
                sp.wait_ge(out_ready, q + 1)
                sp.dma_start(out[:, 4 * q:4 * q + 4, :], X[:, 0, 4 * q:4 * q + 4, :]).then_inc(out_done, 16)
            sp.wait_ge(out_done, 64)

        BULK = (["gt"] + [f"lx{p}" for p in range(4)] + ["k0", "k1"] + [f"v{p}" for p in range(4)] + ["q0", "q1"]
                + [f"lg{p}" for p in range(4)] + ["o0", "o1"] + [f"woa{p}" for p in range(8)]
                + [f"wob{p}" for p in range(8)])
        EXTRA = {1: [("sel",)], 10: [("dec",)], 12: [("tr",)], 20: [("kt",)]}
        for b in range(LRU_N):
            EXTRA.setdefault(2 * b + 3, []).append(("gates", b))
        UPD = [(0, 0, 21), (1, 1, 22), (0, 1, 23), (1, 0, 24), (0, 2, 33), (1, 3, 34)]
        OUTS = [(0, 2, 0, 25), (0, 2, 1, 27), (1, 3, 0, 29), (1, 3, 1, 31),
                (0, 3, 0, 35), (0, 3, 1, 37), (1, 2, 0, 39), (1, 2, 1, 41)]
        for i, (d, c, t) in enumerate(UPD):
            EXTRA.setdefault(t, []).append(("upd", i))
        for i, (d, c, hh, t) in enumerate(OUTS):
            EXTRA.setdefault(t, []).append(("ds", i))
            EXTRA.setdefault(t + 1, []).append(("pv", i))
        EXTRA.setdefault(46, []).append(("ht",))
        ORDER = [e for t in sorted(EXTRA) for e in EXTRA[t]]
        EXT = {e: i for i, e in enumerate(ORDER)}

        def shift(i, s):
            return mod[:, s, 0, :] if i == 0 else modx[:, (3 if s else 1) if i == 1 else 6, :]

        def stat_tile(pe, mm, i, d, n):
            pe.wait_ge(sq_done, DT * i + d + 1)
            mm(ps[:, 7, 0:n], c_("ones"), sq[:, d % 2, 0:n], start=(d == 0), stop=(d == DT - 1)).then_inc(sq_used, 1)

        def bank_of(name):
            return 2 * (BULK.index(name) % 2)

        def unit_done(eng, *unit):
            eng.wait_ge(unit_used, MIX + TICK[unit] + 1)

        @block.tensor
        def _(pe):
            mm = nc.tensor.matmul

            def begin(n_at):
                pe.wait_ge(lo_done, n_at + 1)

            pe.wait_ge(params_in, 32)
            pe.wait_ge(cond_ready, 1)
            for b in range(3):
                for k in range(DT):
                    n = b * DT + k
                    begin(n)
                    for w, cond in ((WH, CH), (WL, CL)):
                        for q in range(4):
                            last = mm(ps[0:4, q, :], cond[:, k, :], w[:, n % 2, q * 512:(q + 1) * 512],
                                      start=(k == 0 and w is WH), stop=(k == DT - 1 and w is WL))
                    last.then_inc(unit_used, 1)
                    if b == 1:
                        stat_tile(pe, mm, 0, k, 512)
                pe.wait_ge(half_free[0], b + 1)
                if b >= 1:
                    pe.wait_ge(half_free[1], b)
                for j in range(DT):
                    last = mm(ps[:, 4, 2 * j:2 * j + 2], rows4[0:4, j * P:(j + 1) * P], c_("comb")[0:4, :],
                              start=True, stop=True)
                last.then_inc(col_done, 1)

            def products(bank, wh, wl, xh, xl, xhl, first, last, lat):
                o = ps[:, bank, :].rearrange("p (s t) -> p s t", s=2)
                if lat:
                    mm(o, wh, xhl, start=first, stop=False)
                    return mm(ps[:, bank, 0:SEQ], wl, xh, start=False, stop=last)
                mm(o, wh, xh, start=first, stop=False)
                mm(o, wh, xl, start=False, stop=False)
                return mm(o, wl, xh, start=False, stop=last)

            def ffn(base, h0, s0, g, lat, sums=False):
                for u in range(12):
                    if sums and u == 1:
                        pe.wait_ge(sums_done, 16 * g + 2)
                        for j in range(DT):
                            last = mm(ps[:, 3, j:j + 1], acc[:, j * P:(j + 1) * P], c_("ones", 0, 1), start=True, stop=True)
                        last.then_inc(late_cols, 1)
                    if sums and u == 2:
                        pe.wait_ge(late_read, g + 1)
                    n = base + u
                    begin(n + 12 * g)
                    turn = u // 4 if u < 8 else u - 6
                    half = turn % 2
                    if u in (0, 4) or u >= 8:
                        pe.wait_ge(half_free[half], h0 + turn // 2 + 3 * g)
                    if u < 8:
                        w1, w2 = wv(WH, n % 2, 8, 256), wv(WL, n % 2, 8, 256)
                        for kk in range(8):
                            k = 8 * (u % 2) + kk
                            if u in (0, 1):
                                pe.wait_ge(xsplit, s0 + k + 1)
                            for ct in range(2):
                                a, z = w1[:, kk, ct * P:(ct + 1) * P], w2[:, kk, ct * P:(ct + 1) * P]
                                bank = 4 * half + 2 * ((u // 2) % 2) + ct
                                if lat:
                                    last = products(bank, a, z, XL2[:, 0, k, :], None, XL2[:, :, k, :],
                                                    k == 0, k == DT - 1, True)
                                else:
                                    last = products(bank, a, z, XHL[:, :, 0, k, :], XHL[:, :, 1, k, :], None,
                                                    k == 0, k == DT - 1, False)
                    else:
                        w1, w2 = wv(WH, n % 2, 4, 512), wv(WL, n % 2, 4, 512)
                        per = 2 if lat else 4
                        for j in range(4):
                            hid = (j // 2 + 1) if lat else (j + 1)
                            if u == 8:
                                pe.wait_ge(hid_ready, (4 * GROUPS if lat else 0) + per * g + hid)
                            for ct in range(4):
                                a, z = w1[:, j, ct * P:(ct + 1) * P], w2[:, j, ct * P:(ct + 1) * P]
                                if lat:
                                    last = products(4 * half + ct, a, z, HHL[:, 0, j, 0:SEQ], None,
                                                    HHL[:, :, j, 0:SEQ], j == 0, j == 3, True)
                                else:
                                    h1 = HHL[:, 0, j, :].rearrange("p (s t) -> p s t", s=2)
                                    h2 = HHL[:, 1, j, :].rearrange("p (s t) -> p s t", s=2)
                                    last = products(4 * half + ct, a, z, h1, h2, None, j == 0, j == 3, False)
                    last.then_inc(unit_used, 1)

            with nc.tensor.Fori(0, 2) as g:
                ffn(FF1, H_FF1, 0, g, False, True)
            with nc.tensor.Fori(2, 8) as g:
                ffn(FF1, H_FF1, 0, g, False, True)
            ffn(FF1, H_FF1, 0, 8, False, True)
            with nc.tensor.Fori(9, GROUPS) as g:
                ffn(FF1, H_FF1, 0, g, False)

            pe.wait_ge(half_free[1], H_FF1 + 3 * GROUPS)
            for d in range(DT):
                stat_tile(pe, mm, 1, d, 512)

            def extra(e):
                i = EXT[e]
                if i >= 1:
                    pe.wait_ge(ext_free, i)
                kind = e[0]
                if kind == "sel":
                    pe.wait_ge(bulk_free[0], 1)
                    for q in range(2):
                        last = mm(ps[0:40, 4 + q, :], c_("sel", 40 * q, 40 * q + 40)[0:32, :], GT, start=True, stop=True)
                elif kind == "gates":
                    b = e[1]
                    pe.wait_ge(conv_done, b + 1)
                    pe.wait_ge(lruw_in, 16 * (b + 1))
                    for q in range(4):
                        last = mm(ps[:, 4 + q, :], LW[:, q, :], xc[:, b % 2, :], start=True, stop=True)
                elif kind == "dec":
                    pe.wait_ge(dec_rhs, 1)
                    last = mm(ps[:, 4, 0:32], c_("parity")[0:40, :], mst[0:40, 16:48], start=True, stop=True)
                elif kind == "tr":
                    pe.wait_ge(exp_rows, 1)
                    src = ([rows[0:40, 0, (2 + c) * P:(3 + c) * P] for c in range(2)]
                           + [rows[0:40, 1, c * P:(c + 1) * P] for c in range(4)]
                           + [rows[0:40, 2, c * P:(c + 1) * P] for c in range(4)])
                    for q, r in enumerate(src):
                        last = nc.tensor.transpose(ps[:, 4, q * 40:(q + 1) * 40], r, c_("ident")[0:40, 0:40])
                elif kind == "kt":
                    for j in range(4):
                        for c in range(2):
                            last = nc.tensor.transpose(ps[:, 4 + j // 2, (j % 2) * 256 + c * P:(j % 2) * 256 + (c + 1) * P],
                                                       knat[:, 2 + c, j * P:(j + 1) * P], c_("ident"))
                elif kind == "upd":
                    d, c, _ = UPD[e[1]]
                    pe.wait_ge(kw_done, e[1] + 1)
                    for j in range(4):
                        last = mm(ps[:, 4 + j, 0:258].rearrange("p (a v) -> p a v", a=2), kw[:, j * P:(j + 1) * P],
                                  vaug[:, c, 2 * j:2 * j + 2, 0:129], start=True, stop=True)
                elif kind == "ds":
                    d, c, hh, _ = OUTS[e[1]]
                    if e[1] == 0:
                        for q in ("q0", "q1"):
                            pe.wait_ge(bulk_free[BULK.index(q) % 2], BULK.index(q) // 2 + 1)
                    for i4 in range(4):
                        h = 4 * hh + i4
                        mm(ps[:, 4, i4 * P:(i4 + 1) * P],
                           c_("ident")[0:40, 32 * d + h:32 * d + h + 1].to_broadcast([40, P]),
                           rows[0:40, 3, c * P:(c + 1) * P], start=True, stop=True)
                        last = mm(ps[:, 5, i4 * P:(i4 + 1) * P], kT[:, h // 2, (c - 2) * P:(c - 1) * P],
                                  qz[:, h % 2, h // 2, (c - 2) * P:(c - 1) * P], start=True, stop=True)
                elif kind == "pv":
                    d, c, hh, _ = OUTS[e[1]]
                    for i4 in range(4):
                        h = 4 * hh + i4
                        col = (i4 % 2) * 129
                        mm(ps[:, 4 + i4 // 2, col:col + 129], Dx[:, i4, :], vaug[:, c, h, 0:129], start=True, stop=True)
                        last = mm(ps[:, 6 + i4 // 2, col:col + 129], qz[:, h % 2, h // 2, (c - 2) * P:(c - 1) * P],
                                  C[:, d, h // 2, (h % 2) * 129:(h % 2) * 129 + 129], start=True, stop=True)
                elif kind == "ht":
                    pe.wait_ge(hn_done, 2)
                    for c in range(2):
                        for h in range(HEADS):
                            last = nc.tensor.transpose(ps[:, 4 + 2 * c + h // 4, (h % 4) * P:(h % 4 + 1) * P],
                                                       Hs[:, c, h, :], c_("ident"))
                last.then_inc(ext_done, 1)

            for i, (kind, p, h) in enumerate(MIX_UNITS):
                n = MIX + i
                begin(n)
                name = kind if kind == "gt" else f"{kind}{p}"
                t = BULK.index(name)
                bank = bank_of(name)
                if h == 0:
                    if t < 2:
                        pe.wait_ge(half_free[0], H_FF1 + 3 * GROUPS)
                    else:
                        pe.wait_ge(bulk_free[t % 2], t // 2)
                s = n % 2
                if kind == "gt":
                    for k in range(DT):
                        pe.wait_ge(xsplit, DT + k + 1)
                        a, z = WH[:, s, k * 32:(k + 1) * 32], WL[:, s, k * 32:(k + 1) * 32]
                        o = ps[0:32, bank, :].rearrange("p (s t) -> p s t", s=2)
                        mm(o, a, XHL[:, :, 0, k, :], start=(k == 0), stop=False)
                        mm(o, a, XHL[:, :, 1, k, :], start=False, stop=False)
                        last = mm(o, z, XHL[:, :, 0, k, :], start=False, stop=(k == DT - 1))
                elif kind in ("lx", "lg", "q", "woa", "wob"):
                    w1, w2 = wv(WH, s, 8, 256), wv(WL, s, 8, 256)
                    if kind == "woa":
                        pe.wait_ge(mxa_done, 1)
                    if kind == "wob":
                        pe.wait_ge(mxb_done, 1)
                    for kk in range(8):
                        k = 8 * h + kk
                        for ct in range(2):
                            a, z = w1[:, kk, ct * P:(ct + 1) * P], w2[:, kk, ct * P:(ct + 1) * P]
                            if kind == "lx":
                                last = products(bank + ct, a, z, XHL[:, :, 0, k, :], XHL[:, :, 1, k, :], None,
                                                k == 0, k == DT - 1, False)
                            elif kind in ("lg", "q"):
                                last = products(bank + ct, a, z, XHL[:, 1, 0, k, :], None, XHL[:, 1, :, k, :],
                                                k == 0, k == DT - 1, True)
                            else:
                                m = MXA if kind == "woa" else MXB
                                last = products(bank + ct, a, z, m[:, 0, kk, :], None, m[:, :, kk, :],
                                                kk == 0, kk == 7, True)
                else:
                    nk, nw, toks = (4, 512, (2, 3)) if kind == "o" else (8, 256, range(4))
                    w1, w2 = wv(WH, s, nk, nw), wv(WL, s, nk, nw)
                    for kk in range(nk):
                        k = nk * h + kk
                        for ti, tt in enumerate(toks):
                            xh, xl = (XHL[:, tt // 2, q, k, (tt % 2) * P:(tt % 2 + 1) * P] for q in range(2))
                            if kind == "o":
                                o = ps[:, bank + ti, :]
                                fresh = True
                            else:
                                o = ps[:, bank + ti // 2, (ti % 2) * 256:(ti % 2 + 1) * 256]
                                fresh = ti % 2 == 0
                            shared = kind != "o"
                            mm(o, xh, w1[:, kk, :], start=(k == 0 and fresh), stop=False, skip_group_check=shared)
                            mm(o, xl, w1[:, kk, :], start=False, stop=False, skip_group_check=shared)
                            last = mm(o, xh, w2[:, kk, :], start=False, stop=(k == DT - 1), skip_group_check=shared)
                last.then_inc(unit_used, 1)
                for e in EXTRA.get(i, []):
                    extra(e)

            pe.wait_ge(ext_free, len(ORDER))
            for d in range(DT):
                stat_tile(pe, mm, 2, d, SEQ)
            for t in (0, 1):
                pe.wait_ge(bulk_free[t], (len(BULK) + 1 - t) // 2)
            with nc.tensor.Fori(0, GROUPS - 1) as g:
                ffn(FF2, H_FF2, 2 * DT, g, True)
            ffn(FF2, H_FF2, 2 * DT, GROUPS - 1, True)
            pe.wait_ge(half_free[1], H_FF2 + 3 * GROUPS)
            for d in range(DT):
                stat_tile(pe, mm, 3, d, SEQ)

        @block.scalar
        def _(act):
            A = nc.scalar.activation

            def split(n, g=None, size=UW):
                m = 0 if g is None else g
                act.wait_ge(stage_full[n % 3], 16 * (n // 3 + 1) + 64 * m)
                if n >= 2:
                    act.wait_ge(unit_used, n - 1 + 12 * m)
                A(WH[:, n % 2, 0:size], stage[:, n % 3, 0:size], ACT.Copy).then_inc(hi_done, 1)

            def squares(i, d, lat):
                if DT * i + d >= 2:
                    act.wait_ge(sq_used, DT * i + d - 1)
                if not lat:
                    A(sq[:, d % 2, 0:256], X[:, 0, d, :], ACT.Square)
                    A(sq[:, d % 2, 256:512], X[:, 1, d, :], ACT.Square).then_inc(sq_done, 1)
                else:
                    A(sq[:, d % 2, 0:256], X[:, 1, d, :], ACT.Square).then_inc(sq_done, 1)

            def root(i, n):
                act.wait_ge(var_ready, i + 1)
                A(rms[:, 0:n], rms[:, 0:n], ACT.Sqrt).then_inc(root_ready, 1)

            def modulate(i, d, lat):
                act.wait_ge(xn_done, DT * i + d + 1)
                if DT * i + d >= 2:
                    act.wait_ge(xsplit, DT * i + d - 1)
                for s in ((1,) if lat else (0, 1)):
                    c = 0 if lat else 256 * s
                    last = A(xm[:, d % 2, c:c + 256], xn[:, d % 2, c:c + 256], ACT.Identity,
                             bias=shift(i, s)[:, d:d + 1], scale=scl[:, i, s, d:d + 1])
                last.then_inc(xm_done, 1)

            act.wait_ge(params_in, 32)
            A(silc[:], v_("c"), ACT.Silu).then_inc(cond_silu, 1)
            act.wait_ge(cond_silu, 1)
            sv = silc[:].rearrange("p (s k) -> p k s", s=2)
            A(CH[:, :, 0:4:2], sv, ACT.Copy)
            act.wait_ge(zeros_set, 1)
            A(CL[:, :, 0:4:2], sv, ACT.Copy).then_inc(cond_silu, 1)
            act.wait_ge(rate_arg, 1)
            A(lsp[:, 1, :], lsp[:, 1, :], ACT.Exp, scale=-1.0).then_inc(rate_exp, 1)
            act.wait_ge(rate_u, 1)
            A(lsp[:, 0, :], lsp[:, 0, :], ACT.Ln).then_inc(rate_ln, 1)

            split(0)
            for b in range(3):
                for k in range(DT):
                    n = b * DT + k
                    split(n + 1)
                    if b == 1:
                        if k == 0:
                            act.wait_ge(x_in, 32)
                        squares(0, k, False)
                    if b == 2:
                        if k == 0:
                            root(0, 512)
                        modulate(0, k, False)
                act.wait_ge(unit_used, n + 1)
                if b >= 1:
                    act.wait_ge(col_done, b)
                A(rows4[0:4, :].rearrange("p (q n) -> p q n", q=4), ps[0:4, 0:4, :], ACT.Copy).then_inc(half_free[0], 1)

            def ffn(base, h0, g, lat, last_group=False):
                e0 = (4 * GROUPS if lat else 0)
                per = 2 if lat else 4
                for u in range(12):
                    if not (last_group and u == 11):
                        split(base + u + 1, g)
                    if u >= 8:
                        continue
                    half = u // 4
                    gate, up = 4 * half, 4 * half + 2
                    if u % 4 == 1:
                        act.wait_ge(unit_used, base + u + 1 + 12 * g)
                        if not lat:
                            if half == 1:
                                act.wait_ge(hid_ready, 4 * g + 2)
                            for ct in range(2):
                                A(G[:, ct, :], ps[:, gate + ct, :], ACT.Silu).then_inc(silu_done, 1)
                        else:
                            act.wait_ge(hid_ready, e0 + 2 * g + half)
                            A(U[:, :, 0:256], ps[:, gate:gate + 2, 256:512], ACT.Copy).then_inc(gate_lo, 1)
                            act.wait_ge(gate_sum, 2 * g + half + 1)
                            A(G[:, :, 0:256], G[:, :, 0:256], ACT.Silu).then_inc(silu_done, 1)
                    if u % 4 == 3:
                        if not lat:
                            for ct in range(2):
                                if ct == 0:
                                    act.wait_ge(prod_done, 2 * g + half + 1)
                                else:
                                    act.wait_ge(half_free[half], h0 + 3 * g + 1)
                                A(HHL[:, 0, 2 * half + ct, :], G[:, ct, :], ACT.Copy).then_inc(hid_hi, 1)
                        else:
                            act.wait_ge(unit_used, base + u + 1 + 12 * g)
                            A(U[:, :, 256:512], ps[:, up:up + 2, 256:512], ACT.Copy).then_inc(up_lo, 1)
                            act.wait_ge(prod_done, 2 * GROUPS + 2 * g + half + 1)
                            A(HHL[:, 0, 2 * half:2 * half + 2, 0:256], G[:, :, 0:256], ACT.Copy).then_inc(hid_hi, 1)

            with nc.scalar.Fori(0, GROUPS) as g:
                ffn(FF1, H_FF1, g, False)

            for t in range(2):
                act.wait_ge(half_free[t], H_FF1 + 3 * GROUPS)
            for d in range(DT):
                squares(1, d, False)
            root(1, 512)
            for d in range(DT):
                modulate(1, d, False)

            def extra_ready(*e):
                act.wait_ge(ext_done, EXT[e] + 1)

            def load_lru(b):
                act.dma_start(LW, lru_w[:, b]).then_inc(lruw_in, 16)

            def tick(i):
                def turn_done(name, *unit):
                    unit_done(act, *unit)
                    return bank_of(name), bulk_free[BULK.index(name) % 2]

                if i == 0:
                    bk, free = turn_done("gt", "gt", 0, 0)
                    A(GT, ps[0:32, bk, :], ACT.Copy).then_inc(free, 1)
                    act.wait_ge(xsplit, 2 * DT)
                    load_lru(0)
                if i == 2:
                    extra_ready("sel")
                    A(rows[0:40, 0, :], ps[0:40, 4, :], ACT.Identity, bias=v_("mg", 0, 1)[0:40, :])
                    A(rows[0:40, 1, :], ps[0:40, 5, :], ACT.Identity, bias=v_("mg", 1, 2)[0:40, :]).then_inc(ext_free, 1)
                    act.wait_ge(ext_free, EXT[("sel",)] + 1)
                    A(rows[0:40, 2, :], rows[0:40, 1, :], ACT.Abs).then_inc(act_step, 1)
                    act.wait_ge(act_step, 1)
                    A(rows[0:40, 2, :], rows[0:40, 2, :], ACT.Exp, scale=-1.0).then_inc(act_step, 1)
                    act.wait_ge(act_step, 2)
                    A(rows[0:40, 2, :], rows[0:40, 2, :], ACT.Ln, bias=c_("one")[0:40, :]).then_inc(log_done, 1)
                if i in (2, 4, 6, 8):
                    p = i // 2 - 1
                    bk, free = turn_done(f"lx{p}", "lx", p, 1)
                    A(xpad[:, 2 * p:2 * p + 2, 0, 2:258], ps[:, bk:bk + 2, 0:256], ACT.Copy)
                    for a in range(2):
                        last = A(xpad[:, 2 * p + a, 1, 2:258].rearrange("p (r c) -> p c r", r=ROWS),
                                 ps[:, bk + a, 256:512].rearrange("p (c r) -> p c r", r=ROWS), ACT.Copy)
                    last.then_inc(free, 1)
                if 3 <= i <= 19:
                    b, phase = divmod(i - 3, 2)
                    if phase == 1 and b < LRU_N:
                        extra_ready("gates", b)
                        if b < LRU_N - 1:
                            load_lru(b + 1)
                        if b >= 1:
                            act.wait_ge(lru_done, b)
                        for d in range(2):
                            A(Rg[:, d, :], ps[:, 4 + 2 * d, :], ACT.Sigmoid, bias=v_("b_r", d * 8 + b, d * 8 + b + 1))
                            A(Ig[:, d, :], ps[:, 5 + 2 * d, :], ACT.Sigmoid,
                              bias=v_("b_i", d * 8 + b, d * 8 + b + 1)).then_inc(act_step, 1)
                        act.wait_ge(act_step, 2 + 2 * (b + 1) + b * 2)
                        for d in range(2):
                            A(Ag[:, d, :], Rg[:, d, :], ACT.Exp, scale=lsp[:, 0, d * 8 + b:d * 8 + b + 1])
                            A(Rg[:, d, :], Rg[:, d, :], ACT.Tanh,
                              scale=lsp[:, 1, d * 8 + b:d * 8 + b + 1]).then_inc(act_step, 1)
                        act.wait_ge(act_step, 2 + 4 * (b + 1))
                        A(ps[:, 4:6, :], Ag, ACT.Square).then_inc(act_a, 1)
                    elif phase == 0:
                        if b >= 1:
                            act.wait_ge(z_done, b)
                            A(Rg, Rg, ACT.Sqrt).then_inc(root_z, 1)
                        if b < LRU_N:
                            if b % 2 == 0:
                                act.wait_ge(bulk_free[BULK.index(f"lx{b // 2}") % 2], BULK.index(f"lx{b // 2}") // 2 + 1)
                            if b >= 2:
                                act.wait_ge(lru_done, b - 1)
                            if b == 0:
                                act.wait_ge(ext_done, EXT[("sel",)] + 1)
                                act.wait_ge(pads_set, 1)
                            A(xc[:, b % 2, :].rearrange("p (s t) -> p s t", s=2), xpad[:, b, :, 0:256], ACT.Identity,
                              bias=v_("conv_b", b, b + 1), scale=v_("conv_w", b, b + 1)).then_inc(conv_first, 1)
                if i == 7:
                    act.wait_ge(enm_arg, 1)
                    for c in (2, 3):
                        A(rows[0:40, 1, (c - 2) * P:(c - 1) * P], rows[0:40, 3, c * P:(c + 1) * P], ACT.Exp,
                          scale=-1.0, bias=mst[0:40, c:c + 1])
                    A(rows[0:40, 1, 256:512], rows[0:40, 1, 256:512], ACT.Exp, scale=-1.0)
                    for c in range(4):
                        A(rows[0:40, 2, c * P:(c + 1) * P], rows[0:40, 0, c * P:(c + 1) * P], ACT.Exp,
                          bias=mst[0:40, 4 + c:5 + c])
                    A(mst[0:40, 8:12], mst[0:40, 8:12], ACT.Exp).then_inc(exp_rows, 1)
                if i in (10, 12):
                    p = (i - 10) // 2
                    bk, free = turn_done(f"k{p}", "k", p, 1)
                    A(knat[:, :, p * 256:(p + 1) * 256],
                      ps[:, bk:bk + 2, :].rearrange("p b (a n) -> p (b a) n", a=2), ACT.Copy,
                      scale=DK ** -0.5).then_inc(free, 1)
                if i in (14, 16, 18, 20):
                    p = (i - 14) // 2
                    bk, free = turn_done(f"v{p}", "v", p, 1)
                    for b2 in range(2):
                        last = A(vaug[:, 2 * b2:2 * b2 + 2, 2 * p:2 * p + 2, 0:DV],
                                 ps[:, bk + b2, :].rearrange("p (a h v) -> p a h v", a=2, h=2), ACT.Copy)
                    last.then_inc(free, 1)
                if i in (22, 24):
                    p = (i - 22) // 2
                    bk, free = turn_done(f"q{p}", "q", p, 1)
                    if p == 1:
                        act.wait_ge(bulk_free[BULK.index("q0") % 2], BULK.index("q0") // 2 + 1)
                    A(Dx[:, 0:2, :].rearrange("p a t -> p (a t)"), ps[:, bk, 256:512], ACT.Copy)
                    A(Dx[:, 2:4, :].rearrange("p a t -> p (a t)"), ps[:, bk + 1, 256:512], ACT.Copy).then_inc(lo_copy, 1)
                for j, (d, c, hh, t) in enumerate(OUTS):
                    if i == t + 1:
                        act.wait_ge(d_masked, j + 1)
                        for i4 in range(4):
                            h = 32 * d + 4 * hh + i4
                            last = A(Dx[:, i4, :], Dx[:, i4, :], ACT.Exp, bias=tr[:, c - 2, h:h + 1])
                        last.then_inc(d_exp, 1)
                    if i == t + 2:
                        extra_ready("pv", j)
                        if j >= 1:
                            act.wait_ge(num_done, j)
                        for i4 in range(4):
                            h = 32 * d + 4 * hh + i4
                            last = A(t1[:, i4, :], ps[:, 6 + i4 // 2, (i4 % 2) * 129:(i4 % 2) * 129 + 129], ACT.Copy,
                                     scale=tr[:, c, h:h + 1])
                        last.then_inc(inter_done, 1)
                if i in (26, 28, 30, 32):
                    p = (i - 26) // 2
                    bk, free = turn_done(f"lg{p}", "lg", p, 1)
                    if p == 0:
                        act.wait_ge(lru_done, LRU_N)
                    A(lgs[:, 2 * p:2 * p + 2, :], ps[:, bk:bk + 2, 256:512], ACT.Copy).then_inc(lo_copy, 1)
                if i == 34:
                    for q in ("lg2", "lg3"):
                        act.wait_ge(bulk_free[BULK.index(q) % 2], BULK.index(q) // 2 + 1)
                    A(lgs, lgs, ACT.Gelu_apprx_tanh).then_inc(gelu_done, 1)
                if i == 36:
                    act.wait_ge(lru_mul, 1)
                    A(MXA[:, 0], lgs, ACT.Copy).then_inc(mxa_hi, 1)
                if i in (36, 40):
                    p = (i - 36) // 4
                    bk, free = turn_done(f"o{p}", "o", p, 3)
                    A(SO[:, :, p * 512:(p + 1) * 512], ps[:, bk:bk + 2, :], ACT.Sigmoid).then_inc(free, 1)
                if i in (41, 44):
                    c = 1 if i == 41 else 0
                    act.wait_ge(hms, 1 + (i == 44))
                    A(mst[:, 48 + 8 * c:56 + 8 * c], mst[:, 48 + 8 * c:56 + 8 * c], ACT.Sqrt, scale=1.0 / DV,
                      bias=c_("eps")).then_inc(hroot, 1)
                if i == 47:
                    act.wait_ge(ext_free, EXT[("ht",)] + 1)
                    A(MXB[:, 0], Hs[:, :, :, :].rearrange("p c h v -> p (c h v)").rearrange("p (h t) -> p h t", h=8),
                      ACT.Copy).then_inc(mxb_hi, 1)

            for i in range(len(MIX_UNITS)):
                split(MIX + i + 1)
                tick(i)

            for t in (0, 1):
                act.wait_ge(bulk_free[t], (len(BULK) + 1 - t) // 2)
            for d in range(DT):
                squares(2, d, True)
            root(2, SEQ)
            for d in range(DT):
                modulate(2, d, True)
            with nc.scalar.Fori(0, GROUPS - 1) as g:
                ffn(FF2, H_FF2, g, True)
            ffn(FF2, H_FF2, GROUPS - 1, True, last_group=True)
            for t in range(2):
                act.wait_ge(half_free[t], H_FF2 + 3 * GROUPS)
            for d in range(DT):
                squares(3, d, True)
            root(3, SEQ)

        @block.gpsimd
        def _(pool):
            unit_done(pool, "v", 3, 1)
            nc.gpsimd.memset(qz[0:64, 1], 0.0)
            nc.gpsimd.memset(qz[64:128, 0], 0.0).then_inc(qz_zero, 1)

        @block.vector
        def _(dve):
            TT, TS, STT = nc.vector.tensor_tensor, nc.vector.tensor_scalar, nc.vector.scalar_tensor_tensor
            steps = [0]

            def link(ins):
                steps[0] += 1
                ins.then_inc(dve_step, 1)
                dve.wait_ge(dve_step, steps[0])

            def split(n, g=0, size=UW):
                dve.wait_ge(hi_done, n + 1 + 12 * g)
                TT(WL[:, n % 2, 0:size], stage[:, n % 3, 0:size], WH[:, n % 2, 0:size].bitcast(F),
                   ALU.subtract).then_inc(lo_done, 1)

            def variance(i, n):
                dve.wait_ge(sq_used, DT * (i + 1))
                TS(rms[:, 0:n], ps[:, 7, 0:n], 1.0 / D_MODEL, EPS, ALU.mult, ALU.add).then_inc(var_ready, 1)

            def inverse(i, n):
                dve.wait_ge(root_ready, i + 1)
                nc.vector.reciprocal(rms[:, 0:n], rms[:, 0:n]).then_inc(rms_ready, 1)
                dve.wait_ge(rms_ready, i + 1)

            def normed(i, d, lat):
                for s in ((1,) if lat else (0, 1)):
                    c = 0 if lat else 256 * s
                    last = TT(xn[:, d % 2, c:c + 256], X[:, s, d, :], rms[:, c:c + 256], ALU.mult)
                last.then_inc(xn_done, 1)

            def x_split(i, d, lat):
                dve.wait_ge(xm_done, DT * i + d + 1)
                n = 256 if lat else 512
                src = xm[:, d % 2, 0:n] if lat else xm[:, d % 2, :].rearrange("p (s t) -> p s t", s=2)
                h = XL2[:, 0, d, :] if lat else XHL[:, :, 0, d, :]
                l = XL2[:, 1, d, :] if lat else XHL[:, :, 1, d, :]
                link(nc.vector.tensor_copy(h, src))
                TT(l, src, h.bitcast(F), ALU.subtract).then_inc(xsplit, 1)

            def norm_tiles(i, lat):
                for d in range(DT + 1):
                    if d < DT:
                        normed(i, d, lat)
                    if d >= 1:
                        x_split(i, d - 1, lat)

            dve.wait_ge(params_in, 32)
            nc.vector.memset(zer[:], 0.0)
            nc.vector.memset(CL[:].bitcast(mybir.dt.uint32), 0).then_inc(zeros_set, 1)
            STT(lsp[:, 1, :], v_("lam"), -1.0, v_("lam"), ALU.mult, ALU.max).then_inc(rate_arg, 1)
            dve.wait_ge(cond_silu, 2)
            sv = silc[:].rearrange("p (s k) -> p k s", s=2)
            TT(CH[:, :, 1:4:2], sv, CH[:, :, 0:4:2].bitcast(F), ALU.subtract).then_inc(cond_ready, 1)

            e_, l_ = lsp[:, 1, :], lsp[:, 0, :]
            u_, z_, m_ = (rate[:, q, :] for q in range(3))
            dve.wait_ge(rate_exp, 1)
            link(TS(u_, e_, 1.0, None, ALU.add))
            link(nc.vector.tensor_copy(l_, u_))
            link(TS(u_, u_, -1.0, None, ALU.add))
            TS(z_, u_, 0.0, None, ALU.is_equal)
            TS(u_, u_, 1e-30, None, ALU.max).then_inc(rate_u, 1)
            dve.wait_ge(rate_u, 1)
            link(nc.vector.reciprocal(u_, u_))
            link(TT(z_, z_, e_, ALU.mult))
            link(TT(u_, u_, e_, ALU.mult))
            dve.wait_ge(rate_ln, 1)
            link(TT(l_, l_, u_, ALU.mult))
            TS(m_, v_("lam"), -1.0, 0.0, ALU.mult, ALU.max)
            link(TT(l_, l_, z_, ALU.add))
            link(TT(l_, l_, m_, ALU.add))
            link(TS(lsp[:, 1, :], l_, 8.0, None, ALU.mult))
            link(TS(lsp[:, 0, :], l_, -8.0, None, ALU.mult))

            split(0)
            for b in range(3):
                for k in range(DT):
                    n = b * DT + k
                    split(n + 1)
                    if b == 2:
                        if k == 0:
                            variance(0, 512)
                            inverse(0, 512)
                        normed(0, k, False)
                        if k >= 1:
                            x_split(0, k - 1, False)
                if b == 2:
                    x_split(0, DT - 1, False)
                dve.wait_ge(col_done, b + 1)
                TT(mod[:, :, b, :], ps[:, 4, 0:32].rearrange("p (j s) -> p s j", s=2),
                   v_("ada_b", b * DT, (b + 1) * DT).rearrange("p (s j) -> p s j", s=1).to_broadcast([P, 2, DT]),
                   ALU.add).then_inc(half_free[1], 1)
                dve.wait_ge(half_free[1], b + 1)
                if b == 1:
                    for s in range(2):
                        last = STT(scl[:, 0, s, :], mod[:, s, 1, :], 1.0, v_("n1"), ALU.add, ALU.mult)
                    link(last)
                if b == 2:
                    link(TS(hgate[:, 0], mod[:, :, 2, :], 0.5, None, ALU.mult))
            nc.vector.memset(acc[:], 0.0).then_inc(sums_done, 2)

            def late_columns(g):
                dve.wait_ge(late_cols, g + 1)
                TT(modx[:, bass.ds(g, 1), :], ps[:, 3:4, 0:DT], v_("ada_bx").rearrange("p (q n) -> p q n", q=9)[:, bass.ds(g, 1), :],
                   ALU.add).then_inc(late_read, 1)

            def ada_sums(g, s, u):
                for k in ADA_TICKS.get(u, ()):
                    c = silc[:, s * DT + k:s * DT + k + 1]
                    dve.wait_ge(ada_full[k % 2], 16 * (k // 2 + 1) + 128 * g)
                    dve.wait_ge(sums_done, 16 * g + k + 2)
                    if k == 0:
                        dve.wait_ge(late_cols, g + 1)
                        TS(acc[:], astage[:, 0, :], c, None, ALU.mult).then_inc(sums_done, 1)
                    else:
                        STT(acc[:], astage[:, k % 2, :], c, acc[:], ALU.mult, ALU.add).then_inc(sums_done, 1)

            def ffn(base, h0, gi, g, lat, last_group=False, columns=False, sums=None):
                for u in range(12):
                    if u >= 1 and sums is not None:
                        ada_sums(g, sums, u - 1)
                    if not (last_group and u == 11):
                        split(base + u + 1, g)
                    n_at = base + u + 1 + 12 * g
                    if columns and u == 0:
                        late_columns(g)
                    half = u // 4
                    gate, up = 4 * half, 4 * half + 2
                    if u % 4 == 1 and u < 8 and lat:
                        dve.wait_ge(gate_lo, 2 * g + half + 1)
                        TT(G[:, :, 0:256], ps[:, gate:gate + 2, 0:256], U[:, :, 0:256], ALU.add).then_inc(gate_sum, 1)
                    if u % 4 == 3 and u < 8:
                        if not lat:
                            dve.wait_ge(unit_used, n_at)
                            for ct in range(2):
                                dve.wait_ge(silu_done, 4 * g + 2 * half + ct + 1)
                                TT(G[:, ct, :], ps[:, up + ct, :], G[:, ct, :], ALU.mult).then_inc(
                                    half_free[half] if ct else prod_done, 1)
                            for ct in range(2):
                                dve.wait_ge(hid_hi, 4 * g + 2 * half + ct + 1)
                                j = 2 * half + ct
                                TT(HHL[:, 1, j, :], G[:, ct, :], HHL[:, 0, j, :].bitcast(F),
                                   ALU.subtract).then_inc(hid_ready, 1)
                        else:
                            dve.wait_ge(up_lo, 2 * g + half + 1)
                            TT(U[:, :, 256:512], ps[:, up:up + 2, 0:256], U[:, :, 256:512],
                               ALU.add).then_inc(half_free[half], 1)
                            dve.wait_ge(half_free[half], h0 + 3 * g + 1)
                            dve.wait_ge(silu_done, 4 * GROUPS + 2 * g + half + 1)
                            TT(G[:, :, 0:256], G[:, :, 0:256], U[:, :, 256:512], ALU.mult).then_inc(prod_done, 1)
                            dve.wait_ge(hid_hi, 4 * GROUPS + 2 * g + half + 1)
                            dve.wait_ge(prod_done, 2 * GROUPS + 2 * g + half + 1)
                            TT(HHL[:, 1, 2 * half:2 * half + 2, 0:256], G[:, :, 0:256],
                               HHL[:, 0, 2 * half:2 * half + 2, 0:256].bitcast(F), ALU.subtract).then_inc(hid_ready, 1)
                    if u >= 8:
                        dve.wait_ge(unit_used, n_at)
                        half = u % 2
                        for part in range(2):
                            for ct in range(4):
                                d = 4 * (u - 8) + ct
                                s = 1 if lat else part
                                last = STT(X[:, s, d, :], ps[:, 4 * half + ct, part * 256:(part + 1) * 256],
                                           hgate[:, gi, s, d:d + 1], X[:, s, d, :], ALU.mult, ALU.add)
                                if lat and part == 0 and ct == 3:
                                    last.then_inc(add_first, 1)
                                    dve.wait_ge(add_first, 4 * g + u - 7)
                        last.then_inc(half_free[half], 1)

            with nc.vector.Fori(0, 2) as g:
                ffn(FF1, H_FF1, 0, g, False, columns=True, sums=0)
            with nc.vector.Fori(2, 8) as g:
                ffn(FF1, H_FF1, 0, g, False, columns=True, sums=1)
            ffn(FF1, H_FF1, 0, 8, False, columns=True)
            with nc.vector.Fori(9, GROUPS) as g:
                ffn(FF1, H_FF1, 0, g, False)
            STT(scl[:, 1, 0, :], modx[:, 2, :], 1.0, v_("n2"), ALU.add, ALU.mult)
            STT(scl[:, 1, 1, :], modx[:, 4, :], 1.0, v_("n2"), ALU.add, ALU.mult)
            STT(scl[:, 2, 1, :], modx[:, 7, :], 1.0, v_("n3"), ALU.add, ALU.mult)
            link(TS(hgate[:, 1, 1, :], modx[:, 8, :], 0.5, None, ALU.mult))

            variance(1, 512)
            inverse(1, 512)
            norm_tiles(1, False)

            def extra_ready(*e):
                dve.wait_ge(ext_done, EXT[e] + 1)

            DIRS = [(0, 0, [0, 1, 2, 3]), (1, 32, [1, 0, 3, 2])]

            def ordered(row, q, c, d):
                v = rows[row:row + 8, q, c * P:(c + 1) * P]
                return v[:, ::-1] if d else v

            def head_cols(q0, c, d):
                return tr[:, q0 + c, 32 * d:32 * d + 8]

            def tick(i):
                if i == 0:
                    nc.vector.memset(xpad[:, :, :, 0:2], 0.0)
                    nc.vector.memset(xpad[:, :, :, 258:260], 0.0).then_inc(pads_set, 1)
                    nc.vector.memset(vaug[:, :, :, DV:VS], 1.0)
                    nc.vector.memset(mst[:], 0.0)
                    link(nc.vector.memset(rows[:, 3, :], 0.0))
                if i == 3:
                    dve.wait_ge(log_done, 1)
                    link(STT(rows[0:40, 1, :], rows[0:40, 1, :], 0.0, rows[0:40, 2, :], ALU.min, ALU.subtract))
                    for d, r, order in DIRS:
                        for c in order:
                            last = nc.vector.tensor_tensor_scan(ordered(r, 2, c, d), ordered(r, 1, c, d), zer[r:r + 8, :],
                                                                0.0, ALU.add, ALU.add)
                    link(last)
                    link(TT(rows[0:40, 0, :], rows[0:40, 0, :], rows[0:40, 2, :], ALU.subtract))
                if i == 4:
                    for t in range(4):
                        for d, r, order in DIRS:
                            c = order[t]
                            last = nc.vector.tensor_tensor_scan(ordered(r, 3, c, d), ordered(r, 0, c, d), ordered(r, 0, c, d),
                                                                mst[r:r + 8, c:c + 1], ALU.max, ALU.max)
                        link(last)
                        if t < 3:
                            for d, r, order in DIRS:
                                e = order[t] * P + (0 if d else P - 1)
                                nxt = order[t + 1]
                                last = TT(mst[r:r + 8, nxt:nxt + 1], rows[r:r + 8, 2, e:e + 1],
                                          rows[r:r + 8, 3, e:e + 1], ALU.add)
                            link(last)
                if i == 5:
                    for d, r, _ in DIRS:
                        m = rows[r:r + 8, 3, :].rearrange("p (c t) -> p c t", c=4)[:, :, (0 if d else P - 1)]
                        last = TS(mst[r:r + 8, 4:8], m, -1.0, None, ALU.mult)
                    link(last)
                    TT(mst[0:40, 8:12], mst[0:40, 0:4], mst[0:40, 4:8], ALU.add)
                    TT(rows[0:40, 1, 256:512], rows[0:40, 2, 256:512], rows[0:40, 3, 256:512],
                       ALU.add).then_inc(enm_arg, 1)
                if i == 8:
                    dve.wait_ge(exp_rows, 1)
                    TT(mst[0:40, 16:48].rearrange("p (d c j) -> p d c j", d=2, c=4),
                       c_("jj")[0:40, :].rearrange("p (d c j) -> p d c j", d=2, c=4),
                       mst[0:40, 8:12].rearrange("p (d c j) -> p d c j", d=1, j=1).to_broadcast([40, 2, 4, 4]),
                       ALU.mult).then_inc(dec_rhs, 1)
                if i == 11:
                    extra_ready("dec")
                    nc.vector.tensor_copy(dec, ps[:, 4, 0:32]).then_inc(ext_free, 1)
                if i == 13:
                    extra_ready("tr")
                    nc.vector.tensor_copy(tr, ps[:, 4, 0:400].rearrange("p (q n) -> p q n", q=10)).then_inc(ext_free, 1)
                    dve.wait_ge(ext_free, EXT[("tr",)] + 1)
                if 3 <= i <= 19:
                    b, phase = divmod(i - 3, 2)
                    if phase == 0:
                        if b >= 1:
                            bb = b - 1
                            dve.wait_ge(root_z, b)
                            link(TT(Ig, Ig, Rg, ALU.mult))
                            nc.vector.tensor_tensor_scan(Rg[:, 0, :], Ag[:, 0, :], Ig[:, 0, :], 0.0, ALU.mult, ALU.add)
                            link(nc.vector.tensor_tensor_scan(
                                Rg[:, 1, 0:256][:, ::-1], Ag[:, 1, 0:256][:, ::-1], Ig[:, 1, 0:256][:, ::-1],
                                0.0, ALU.mult, ALU.add))
                            link(nc.vector.tensor_tensor_scan(
                                Rg[:, 1, 256:512][:, ::-1], Ag[:, 1, 256:512][:, ::-1], Ig[:, 1, 256:512][:, ::-1],
                                Rg[:, 1, 0:1], ALU.mult, ALU.add))
                            TT(LO[:, bb, :], Rg[:, 0, 256:512], Rg[:, 1, 256:512], ALU.add).then_inc(lru_done, 1)
                        if b < LRU_N:
                            dve.wait_ge(conv_first, b + 1)
                            v = xc[:, b % 2, :].rearrange("p (s t) -> p s t", s=2)
                            for k in range(1, 4):
                                ins = STT(v, xpad[:, b, :, k:k + 256], v_("conv_w", k * 8 + b, k * 8 + b + 1), v,
                                          ALU.mult, ALU.add)
                                if k < 3:
                                    link(ins)
                            ins.then_inc(conv_done, 1)
                    elif b < LRU_N:
                        dve.wait_ge(act_a, b + 1)
                        STT(Rg, ps[:, 4:6, :], 1.0, Rg, ALU.add, ALU.mult).then_inc(ext_free, 1)
                        TT(Ig, Ig, xc[:, b % 2:b % 2 + 1, :].to_broadcast([P, 2, 512]), ALU.mult).then_inc(z_done, 1)
                if i == 21:
                    extra_ready("kt")
                    nc.vector.tensor_copy(kT, ps[:, 4:6, :].rearrange("p b (j t) -> p (b j) t", j=2)).then_inc(ext_free, 1)
                if i in (22, 24):
                    p = (i - 22) // 2
                    bk = bank_of(f"q{p}")
                    dve.wait_ge(lo_copy, p + 1)
                    if p == 0:
                        dve.wait_ge(qz_zero, 1)
                    src = ps[:, bk:bk + 2, 0:256]
                    lo = Dx.rearrange("p a t -> p (a t)").rearrange("p (a t) -> p a t", a=2)
                    TT(qz[0:64, 0, 2 * p:2 * p + 2, :], src[0:64], lo[0:64], ALU.add)
                    TT(qz[64:128, 1, 2 * p:2 * p + 2, :], src[64:128], lo[64:128], ALU.add).then_inc(
                        bulk_free[BULK.index(f"q{p}") % 2], 1)
                for j, (d, c, t) in enumerate(UPD):
                    if i == t + 1:
                        extra_ready("upd", j)
                        first = c == (1 if d else 0)
                        if first:
                            nc.vector.tensor_copy(C[:, d], ps[:, 4:8, 0:258]).then_inc(ext_free, 1)
                        else:
                            for jj in range(4):
                                e = d * 16 + c * 4 + jj
                                last = STT(C[:, d, jj, :], C[:, d, jj, :], dec[:, e:e + 1], ps[:, 4 + jj, 0:258],
                                           ALU.mult, ALU.add)
                            last.then_inc(ext_free, 1)
                        dve.wait_ge(ext_free, EXT[("upd", j)] + 1)
                for j, (d, c, t) in enumerate(UPD):
                    if i == t:
                        TT(kw.rearrange("p (h n) -> p h n", h=8), knat[:, c, :].rearrange("p (h n) -> p h n", h=8),
                           tr[:, 6 + c, 32 * d:32 * d + 8].rearrange("p (h n) -> p h n", n=1).to_broadcast([P, 8, 64]),
                           ALU.mult).then_inc(kw_done, 1)
                for j, (d, c, hh, t) in enumerate(OUTS):
                    if i == t + 1:
                        extra_ready("ds", j)
                        msk = c_("maskb" if d else "maskf").rearrange("p (h t) -> p h t", h=1).to_broadcast([P, 4, P])
                        TT(Dx, msk, ps[:, 4, :].rearrange("p (h t) -> p h t", h=4), ALU.subtract).then_inc(d_masked, 1)
                        dve.wait_ge(d_exp, j + 1)
                        TT(Dx, Dx, ps[:, 5, :].rearrange("p (h t) -> p h t", h=4), ALU.mult).then_inc(ext_free, 1)
                    if i == t + 2:
                        dve.wait_ge(inter_done, j + 1)
                        tv = t1.rearrange("p (b i) v -> p b (i v)", b=2)
                        TT(tv, tv, ps[:, 4:6, 0:258], ALU.add).then_inc(ext_free, 1)
                        dve.wait_ge(ext_free, EXT[("pv", j)] + 1)
                        dn = mst[:, 64:68]
                        link(STT(dn, t1[:, :, 128], -1.0, t1[:, :, 128], ALU.mult, ALU.max))
                        link(TT(dn, dn, tr[:, 2 + c, 32 * d + 4 * hh:32 * d + 4 * hh + 4], ALU.max))
                        link(nc.vector.reciprocal(dn, dn))
                        db = dn.rearrange("p (h v) -> p h v", v=1).to_broadcast([P, 4, DV])
                        dst = Hs[:, c - 2, 4 * hh:4 * hh + 4, :]
                        if (d, c) in ((0, 2), (1, 3)):
                            TT(dst, t1[:, :, 0:DV], db, ALU.mult).then_inc(num_done, 1)
                        else:
                            link(TT(t1[:, :, 0:DV], t1[:, :, 0:DV], db, ALU.mult))
                            TT(dst, dst, t1[:, :, 0:DV], ALU.add).then_inc(num_done, 1)
                if i in (26, 28, 30, 32):
                    p = (i - 26) // 2
                    bk = bank_of(f"lg{p}")
                    dve.wait_ge(lo_copy, 2 + p + 1)
                    TT(lgs[:, 2 * p:2 * p + 2, :], ps[:, bk:bk + 2, 0:256], lgs[:, 2 * p:2 * p + 2, :], ALU.add).then_inc(
                        bulk_free[BULK.index(f"lg{p}") % 2], 1)
                if i == 35:
                    dve.wait_ge(gelu_done, 1)
                    v = lgs.rearrange("p b (c r) -> p b c r", r=ROWS)
                    TT(v, v, LO.rearrange("p b (r c) -> p b c r", r=ROWS), ALU.mult).then_inc(lru_mul, 1)
                if i == 37:
                    dve.wait_ge(mxa_hi, 1)
                    TT(MXA[:, 1], lgs, MXA[:, 0].bitcast(F), ALU.subtract).then_inc(mxa_done, 1)
                if i in (40, 44):
                    c = 1 if i == 40 else 0
                    q = lgs.rearrange("p b t -> p (b t)")[:, 0:1024].rearrange("p (h v) -> p h v", h=8)
                    dve.wait_ge(mxa_done, 1)
                    dve.wait_ge(num_done, 6 if c else 8)
                    link(TT(q, Hs[:, c], Hs[:, c], ALU.mult))
                    nc.vector.reduce_sum(mst[:, 48 + 8 * c:56 + 8 * c], q, AX.X).then_inc(hms, 1)
                if i in (41, 45):
                    c = 1 if i == 41 else 0
                    dve.wait_ge(hroot, 1 + (i == 45))
                    r = mst[:, 48 + 8 * c:56 + 8 * c]
                    link(nc.vector.reciprocal(r, r))
                    link(TT(Hs[:, c], Hs[:, c], r.rearrange("p (h v) -> p h v", v=1).to_broadcast([P, 8, DV]), ALU.mult))
                    for q in ("o0", "o1"):
                        dve.wait_ge(bulk_free[BULK.index(q) % 2], BULK.index(q) // 2 + 1)
                    TT(Hs[:, c], Hs[:, c], SO[:, c].rearrange("p (h v) -> p h v", h=8), ALU.mult).then_inc(hn_done, 1)
                if i == 47:
                    extra_ready("ht")
                    m32 = Hs.rearrange("p c h v -> p (c h v)").rearrange("p (h c t) -> p h c t", h=8, c=2)
                    for c in range(2):
                        last = TT(m32[:, :, c, :], ps[:, 4 + 2 * c:6 + 2 * c, :].rearrange("p b (h t) -> p (b h) t", h=4),
                                  v_("mnorm").rearrange("p (h t) -> p h t", t=1).to_broadcast([P, 8, P]), ALU.mult)
                    last.then_inc(ext_free, 1)
                if i == 48:
                    dve.wait_ge(mxb_hi, 1)
                    TT(MXB[:, 1], Hs.rearrange("p c h v -> p (c h v)").rearrange("p (h t) -> p h t", h=8),
                       MXB[:, 0].bitcast(F), ALU.subtract).then_inc(mxb_done, 1)
                if i >= 41:
                    kind, p, _ = MIX_UNITS[i]
                    name = f"{kind}{p}"
                    bk = bank_of(name)
                    unit_done(dve, kind, p, 0)
                    for part in range(2):
                        for ct in range(2):
                            d = 2 * p + ct
                            last = STT(X[:, 1, d, :], ps[:, bk + ct, part * 256:(part + 1) * 256],
                                       modx[:, 5, d:d + 1], X[:, 1, d, :], ALU.mult, ALU.add)
                        if part == 0:
                            link(last)
                    last.then_inc(bulk_free[BULK.index(name) % 2], 1)

            for i in range(len(MIX_UNITS)):
                split(MIX + i + 1)
                tick(i)

            variance(2, SEQ)
            inverse(2, SEQ)
            norm_tiles(2, True)
            with nc.vector.Fori(0, GROUPS - 1) as g:
                ffn(FF2, H_FF2, 1, g, True)
            ffn(FF2, H_FF2, 1, GROUPS - 1, True, last_group=True)

            variance(3, SEQ)
            inverse(3, SEQ)
            for d in range(DT):
                ins = STT(X[:, 0, d, :], X[:, 1, d, :], v_("nf", d, d + 1), rms[:, 0:SEQ], ALU.mult, ALU.mult)
                if d % 4 == 3:
                    ins.then_inc(out_ready, 1)


_NAMES = ["xT", "vec", "cst", "lru_w", "ada_w", "w_up1", "w_dn1", "w_in", "w_out", "w_up2", "w_dn2"]


def constants():
    import numpy as np

    k = np.zeros((P, NCST), np.float32)

    def put(name, rows, value):
        lo, hi = CST[name]
        k[0:rows, lo:hi] = value

    t = np.arange(P)
    put("ident", P, np.eye(P))
    put("maskf", P, np.where(t[:, None] <= t[None, :], 0.0, -1e30))
    put("maskb", P, np.where(t[:, None] >= t[None, :], 0.0, -1e30))
    put("ones", P, 1.0)
    put("one", P, 1.0)
    put("eps", P, EPS)
    r = np.arange(40)
    live = (r < 8) | (r >= 32)
    put("parity", 40, (live[:, None] & ((r[:, None] % 2) == (t[None, :] >= 64))))
    jj = np.zeros((40, 2, 4, 4))
    sel = np.zeros((32, 2, 40))
    for h in range(HEADS):
        for d in range(2):
            jj[32 * d + h, d, :, h // 2] = 1
            sel[16 * d + h, 0, 32 * d + h] = 1
            sel[16 * d + 8 + h, 1, 32 * d + h] = 1
    put("jj", 40, jj.reshape(40, 32))
    put("sel", 32, sel.reshape(32, 80))
    put("comb", 4, np.array([[1, 0], [1, 0], [0, 1], [0, 1]]))
    return k


def kernel(**inp):
    import numpy as np
    import concourse.bacc as bacc
    from concourse import mybir as mb
    from concourse.bass_utils import run_bass_kernel_spmd

    a = {k: np.asarray(v) for k, v in inp.items()}

    def cols(v):
        return np.ascontiguousarray(v.reshape(-1, P).T)

    lat = a["x"][0].reshape(ROWS, GRID_W, D_MODEL).transpose(1, 0, 2).reshape(SEQ, D_MODEL)
    xT = np.concatenate([v.T.reshape(DT, P, SEQ).transpose(1, 0, 2) for v in (a["ctx"][0], lat)], axis=1)
    mg = np.zeros((P, 2), a["b_mgate"].dtype)
    gates = a["b_mgate"][0].reshape(2, 2, HEADS)
    for d in range(2):
        for q in range(2):
            mg[32 * d:32 * d + HEADS, q] = gates[d, q]
    ada_b = cols(a["ada_b"][0])
    vec = np.concatenate([
        ada_b, np.concatenate([ada_b[:, 0:DT]] + [ada_b[:, b * DT:(b + 1) * DT] for _, b in LATE], axis=1), cols(a["ffn1_norm"][0]), cols(a["mix_norm"][0]), cols(a["ffn2_norm"][0]),
        cols(a["final_norm"]), cols(a["lru_conv_w"][0].reshape(-1)), cols(a["lru_conv_b"][0]),
        cols(a["lru_b_r"][0].reshape(-1)), cols(a["lru_b_i"][0].reshape(-1)), cols(a["lru_lam"][0].reshape(-1)),
        cols(a["c_ctx"]), cols(a["c"][0]), mg, cols(a["mlstm_norm"][0])], axis=1)
    lru_w = np.stack([a["lru_w_r"][0, 0], a["lru_w_i"][0, 0], a["lru_w_r"][0, 1], a["lru_w_i"][0, 1]]).transpose(2, 1, 0, 3)
    arrays = {"xT": xT, "vec": vec, "cst": constants(), "lru_w": lru_w, "ada_w": a["ada_w"][0],
              "w_up1": a["ffn1_w_up"][0], "w_dn1": a["ffn1_w_down"][0], "w_in": a["w_in"][0], "w_out": a["w_out"][0],
              "w_up2": a["ffn2_w_up"][0], "w_dn2": a["ffn2_w_down"][0]}
    arrays = {k: np.ascontiguousarray(v) for k, v in arrays.items()}
    nc = bacc.Bacc("TRN2", target_bir_lowering=False, num_devices=1, dynamic_dma_scratch_size=1024)
    aps = [nc.dram_tensor(f"in_{k}", arrays[k].shape, mb.dt.from_np(arrays[k].dtype), kind="ExternalInput").ap()
           for k in _NAMES]
    out = nc.dram_tensor("out_y", (P, DT, SEQ), mb.dt.float32, kind="ExternalOutput").ap()
    hybrid_layer(nc, *aps, out)
    r = run_bass_kernel_spmd(nc, [{f"in_{k}": arrays[k] for k in _NAMES}], core_ids=[0])
    y = r.results[0]["out_y"]
    y = y.transpose(2, 1, 0).reshape(GRID_W, ROWS, D_MODEL).transpose(1, 0, 2).reshape(1, SEQ, D_MODEL)
    return np.ascontiguousarray(y)
```

```python
import concourse.bass as bass
from concourse import mybir
from contextlib import ExitStack

P = 128
D_MODEL, D_FF, N_MOD = 2048, 5632, 9
SEQ = CTX = 256
GRID_W = 64
ROWS = SEQ // GRID_W
DT = D_MODEL // P
HEADS, DK, DV = 8, 64, 128
LRU_N = 8
EPS = 1e-6
LX0, LG0, Q0, K0, V0, O0, GT0 = 0, 1024, 2048, 2560, 3072, 4096, 5120
GROUPS = D_FF // 512
UW = 2048
VS = 129

LATE = [(0, 3), (0, 4), (1, 3), (1, 4), (1, 5), (1, 6), (1, 7), (1, 8)]
_COLS = [("ada_b", N_MOD * DT), ("ada_bx", (len(LATE) + 1) * DT), ("n1", DT), ("n2", DT), ("n3", DT), ("nf", DT), 
         ("conv_w", 32), ("conv_b", 8), ("b_r", 16), ("b_i", 16), ("lam", 16), ("c", 2 * DT), ("mg", 2), ("mnorm", 8)]
_CONST = [("ident", P), ("maskf", P), ("maskb", P), ("ones", P), ("parity", P), ("jj", 32), ("sel", 80), ("comb", 2),
          ("one", 1), ("eps", 1)]


def _offsets(cols):
    at, out = 0, {}
    for name, n in cols:
        out[name] = (at, at + n)
        at += n
    return out, at


VEC, NVEC = _offsets(_COLS)
CST, NCST = _offsets(_CONST)


def hybrid_layer(nc, xT, vec, cst, lru_w, ada_w, w_up1, w_dn1, w_in, w_out, w_up2, w_dn2, out):
    F, R = mybir.dt.float32, mybir.dt.float32r
    ACT, ALU, AX = mybir.ActivationFunctionType, mybir.AluOpType, mybir.AxisListType

    PAIRS = 2 * DT // 2
    FIRST = PAIRS
    GROUP0 = ["a", 0, "a", "n", "n", 1, "a", "n", "a", "n", "a", "n", 2, "a", "n", "a", "n", "a", "n", 3,
              4, 5, 6, 7, 8, 9, 10, 11]
    assert sum(e in ("a", "n") for e in GROUP0) == DT
    FF1 = FIRST + len(GROUP0)
    AT0 = [FIRST + i for i, e in enumerate(GROUP0) if e not in ("a", "n")]
    ATA = [FIRST + i for i, e in enumerate(GROUP0) if e in ("a", "n")]
    UNSPLIT = [FIRST + i for i, e in enumerate(GROUP0) if e == "n"]
    MIX = FF1 + 12 * (GROUPS - 1)
    MIX_UNITS = ([("lx", 0, 0), ("lx", 0, 1), ("gt", 0, 0)] + [("lx", p, h) for p in range(1, 4) for h in range(2)]
                 + [("k", p, h) for p in range(2) for h in range(2)] + [("v", p, h) for p in range(4) for h in range(2)]
                 + [("q", p, h) for p in range(2) for h in range(2)] + [("lg", p, h) for p in range(4) for h in range(2)]
                 + [("o", p, h) for p in range(2) for h in range(4)]
                 + [("woa", p, 0) for p in range(8)] + [("wob", p, 0) for p in range(8)])
    FF2 = MIX + len(MIX_UNITS)
    UNITS = FF2 + 12 * GROUPS
    TICK = {u: i for i, u in enumerate(MIX_UNITS)}

    ctx = ExitStack()
    with ctx:
        def sb(name, shape, dt=F, scope=ctx):
            return scope.enter_context(nc.sbuf_tensor(name, shape, dt))

        V = sb("vectors", [P, NVEC])
        K = sb("constants", [P, NCST])
        mod = sb("mod", [P, 2, 3, DT])
        modx = sb("mod_late", [P, 9, DT])
        scl = sb("norm_scale", [P, 3, 2, DT])
        hgate = sb("half_gate", [P, 2, 2, DT])
        silc = sb("silu_c", [P, 2 * DT])
        CH = sb("cond_hi", [P, DT, 4], R)
        CL = sb("cond_hi_only", [P, DT, 4], R)
        CF = sb("cond", [P, DT, 4])
        X = sb("residual", [P, 2, DT, SEQ])
        stage = sb("stage", [P, 3, UW])
        WH = sb("w_hi", [P, 2, UW], R)
        WL = sb("w_lo", [P, 2, UW], R)
        lsp = sb("lru_rate", [P, 2, 16])
        rate = sb("rate_work", [P, 3, 16])
        zer = sb("zeros", [P, P])

        with ExitStack() as s1:
            xn1 = sb("normed1", [P, 2, DT, SEQ], F, s1)
            early = sb("early_rows", [P, 3, 2, UW], F, s1)
        with ExitStack() as s1:
            XHL = sb("x_hi_lo", [P, 2, 2, DT, SEQ], R, s1)
            with ExitStack() as s2:
                HHL = sb("hidden_hi_lo", [P, 2, 4, 512], R, s2)
                G = sb("gate_act", [P, 2, 512], F, s2)
                U = sb("up_sum", [P, 2, 512], F, s2)
                with ExitStack() as s3:
                    sq = sb("squares", [P, 2, 512], F, s3)
                    sqs = sb("square_sums", [P, 512], F, s3)
                    rms = sb("rms", [P, 512], F, s3)
                    xn = sb("normed", [P, 4, 512], F, s3)
                    xm = xn[:, 2:4, :]
                    rows4 = sb("ada_rows", [4, UW], F, s3)
                with ExitStack() as s3:
                    acc = sb("ada_sums", [P, UW], F, s3)
                    astage = sb("ada_stage", [P, 2, UW], F, s3)
            with ExitStack() as s2:
                mixA = sb("mixer_pool", [P, 32 * VS + 3 * 2048 + 516 + 512 + 400 + 32 + 68], F, s2)
                with ExitStack() as s3:
                    xpad = sb("conv_in", [P, LRU_N, 2, 260], F, s3)
                with ExitStack() as s3:
                    MXA = sb("mix_lru_hi_lo", [P, 2, 8, SEQ], R, s3)
        with ExitStack() as s1:
            scr = sb("mixer_scratch", [P, 8192], F, s1)
            MXB = sb("mix_mlstm_hi_lo", [P, 2, 8, SEQ], R, s1)
        with ExitStack() as s1:
            XL2 = sb("x2_hi_lo", [P, 2, DT, SEQ], R, s1)

        def carve(pool, sizes):
            at, out = 0, []
            for n in sizes:
                out.append(pool[:, at:at + n])
                at += n
            return out

        vaug, knat, LO, rows, LW, kw, tr, dec, mst = carve(
            mixA, [4 * 8 * VS, 4 * 512, 8 * 256, 4 * 512, 516, 512, 400, 32, 68])
        vaug = vaug.rearrange("p (c h v) -> p c h v", c=4, h=8)
        knat = knat.rearrange("p (c n) -> p c n", c=4)
        LO = LO.rearrange("p (b t) -> p b t", b=8)
        rows = rows.rearrange("p (q t) -> p q t", q=4)
        t1 = LW[:, 0:4 * 129].rearrange("p (h v) -> p h v", h=4)
        LW = LW[:, 0:512].rearrange("p (g n) -> p g n", g=4)
        tr = tr.rearrange("p (q n) -> p q n", q=10)
        kT, qz, C, Hs, Dx = carve(scr, [4 * 256, 2 * 4 * 256, 2 * 4 * 258, 2 * 8 * P, 512])
        kT = kT.rearrange("p (j t) -> p j t", j=4)
        qz = qz.rearrange("p (a j t) -> p a j t", a=2, j=4)
        C = C.rearrange("p (d j n) -> p d j n", d=2, j=4)
        Hs = Hs.rearrange("p (c h v) -> p c h v", c=2, h=8)
        Dx = Dx.rearrange("p (h t) -> p h t", h=4)
        late = X[:, 0, :, :].rearrange("p k t -> p (k t)")
        Rg, Ig, Ag, xc = carve(late, [1024, 1024, 1024, 1024])
        Rg = Rg.rearrange("p (d t) -> p d t", d=2)
        Ig = Ig.rearrange("p (d t) -> p d t", d=2)
        Ag = Ag.rearrange("p (d t) -> p d t", d=2)
        xc = xc.rearrange("p (a t) -> p a t", a=2)
        GT = xc[0:32, 1, :]
        lgs, SO = carve(late, [2048, 2048])
        lgs = lgs.rearrange("p (b t) -> p b t", b=8)
        SO = SO.rearrange("p (c n) -> p c n", c=2)

        ps = ctx.enter_context(nc.psum_tensor("psum", [P, 8, 512], F))

        def v_(name, a=0, b=None):
            lo, hi = VEC[name]
            return V[:, lo + a:(hi if b is None else lo + b)]

        def c_(name, a=0, b=None):
            lo, hi = CST[name]
            return K[:, lo + a:(hi if b is None else lo + b)]

        def sem(name):
            return ctx.enter_context(nc.semaphore(name))

        params_in, x_in, lruw_in, out_ready, out_done = (sem(n) for n in (
            "params_in", "x_in", "lruw_in", "out_ready", "out_done"))
        stage_full = [sem(f"stage_full{i}") for i in range(3)]
        hi_done, lo_done, unit_used = sem("hi_done"), sem("lo_done"), sem("unit_used")
        half_free = [sem("psum_lo_free"), sem("psum_hi_free")]
        zeros_set, cond_silu, cond_ready = sem("zeros_set"), sem("cond_silu"), sem("cond_ready")
        col_done, sq_done, sq_used, root_ready, rms_ready = (sem(n) for n in (
            "col_done", "sq_done", "sq_used", "root_ready", "rms_ready"))
        xn_done, xm_done, xsplit = sem("xn_done"), sem("xm_done"), sem("x_split")
        gate_lo, gate_sum, silu_done, up_lo, prod_done, hid_hi, hid_ready = (sem(n) for n in (
            "gate_lo", "gate_sum", "silu_done", "up_lo", "prod_done", "hid_hi", "hid_ready"))
        dve_step, act_step, add_first = sem("dve_step"), sem("act_step"), sem("add_first")
        log_done, enm_arg, exp_rows, dec_rhs = (sem(n) for n in (
            "log_done", "enm_arg", "exp_rows", "dec_rhs"))
        conv_first, conv_done, act_a, z_done, root_z, lru_done = (sem(n) for n in (
            "conv_first", "conv_done", "lru_act_a", "lru_z", "lru_root", "lru_done"))
        rate_arg, rate_exp, rate_u, rate_ln = sem("rate_arg"), sem("rate_exp"), sem("rate_u"), sem("rate_ln")
        qz_zero, lo_copy, kw_done = (sem(n) for n in (
            "qz_zero", "lo_copy", "kw_done"))
        d_masked, d_exp, inter_done, num_done = (sem(n) for n in (
            "d_masked", "d_exp", "inter_done", "num_done"))
        gelu_done, lru_mul, mxa_hi, mxa_done = (sem(n) for n in (
            "gelu_done", "lru_mul", "mxa_hi", "mxa_done"))
        hms, hroot, hn_done, mxb_hi, mxb_done = (sem(n) for n in (
            "head_ms", "head_root", "head_normed", "mxb_hi", "mxb_done"))
        pads_set = sem("pads_set")
        early_full = [sem(f"early_full{i}") for i in range(3)]
        cols_read, stat_done, scl_ready = sem("cols_read"), sem("stat_done"), sem("norm_scale_ready")
        sum_zero = sem("sum_zero")
        ada_full = [sem("ada_full0"), sem("ada_full1")]
        sums_done, late_cols, late_read = sem("ada_sums_done"), sem("late_cols"), sem("late_read")
        bulk_free = [sem("bulk0_free"), sem("bulk1_free")]
        ext_done, ext_free = sem("ext_done"), sem("ext_free")
        block = ctx.enter_context(nc.Block())

        H_FF1 = (2, 1)
        H_FF2 = tuple(h + 3 * GROUPS for h in H_FF1)

        SPLIT_AFTER = {7: FIRST + 2, 11: FIRST + 5}
        LAST_EARLY = max(SPLIT_AFTER.values())

        def splits(n):
            return n + 1 - sum(m <= n for m in UNSPLIT)

        def half_slot(n):
            return (splits(n) - 1) % 2

        def slot_before(n):
            return [m for m in range(n) if m not in UNSPLIT][-2]

        def slot(n):
            return (n - FIRST) % 3

        ADA_TICKS = {1: (0, 1), 2: (2, 3), 3: (4, 5), 4: (6, 7), 5: (8, 9), 6: (10, 11),
                     7: (12,), 8: (13,), 9: (14,), 10: (15,)}
        assert [k for t in sorted(ADA_TICKS) for k in ADA_TICKS[t]] == list(range(DT))

        def unit_src(i):
            kind, p, h = MIX_UNITS[i]
            if kind == "gt":
                return w_in[:, GT0:GT0 + 32].rearrange("(k p) c -> p k c", p=P), 16, 32
            if kind == "o":
                return w_in[h * 512:(h + 1) * 512, O0 + p * 512:O0 + (p + 1) * 512].rearrange(
                    "(k p) c -> p k c", p=P), 4, 512
            if kind in ("woa", "wob"):
                r = 1024 * (kind == "wob")
                return w_out[r:r + 1024, p * 256:(p + 1) * 256].rearrange("(k p) c -> p k c", p=P), 8, 256
            c = {"lx": LX0, "k": K0, "v": V0, "q": Q0, "lg": LG0}[kind] + p * 256
            return w_in[h * 1024:(h + 1) * 1024, c:c + 256].rearrange("(k p) c -> p k c", p=P), 8, 256

        def wv(w, slot, k, c):
            return w[:, slot, 0:k * c].rearrange("p (k c) -> p k c", k=k)

        @block.sync
        def _(sp):
            sp.dma_start(V[:], vec).then_inc(params_in, 16)
            sp.dma_start(K[:], cst).then_inc(params_in, 16)

            def load(n, k, c, src, at):
                if n >= FIRST + 3:
                    if n - 3 in UNSPLIT:
                        sp.wait_ge(unit_used, n - 2)
                    else:
                        sp.wait_ge(lo_done, splits(n - 3) + at - n)
                sp.dma_start(wv(stage, slot(n), k, c), src).then_inc(stage_full[slot(n)], 16)

            for n in range(PAIRS):
                b, p = divmod(n, DT // 2)
                if n >= 3:
                    sp.wait_ge(unit_used, n - 2)
                sp.dma_start(early[:, n % 3], ada_w[2 * p * P:(2 * p + 2) * P, b * UW:(b + 1) * UW].rearrange(
                    "(k p) c -> p k c", p=P)).then_inc(early_full[n % 3], 16)
                if n == 1:
                    for s in range(2):
                        sp.dma_start(X[:, s], xT[:, s * DT:(s + 1) * DT, :]).then_inc(x_in, 16)

            def ffn_loads(base, w_up, w_dn, g, g_at):
                for u in range(12):
                    if base is None:
                        n = AT0[u]
                        for a in (a for a in ATA if (AT0[u - 1] if u else 0) < a < n):
                            k = ATA.index(a)
                            load(a, 1, UW, ada_w[k * P:(k + 1) * P, 2 * UW:3 * UW].rearrange("(k p) c -> p k c", p=P), a)
                    else:
                        n = base + u
                    if u < 8:
                        half, up, kh = u // 4, (u // 2) % 2, u % 2
                        c = up * D_FF + half * 256
                        src = w_up[kh * 1024:(kh + 1) * 1024, bass.ds(g * 512 + c, 256)].rearrange(
                            "(k p) c -> p k c", p=P)
                        load(n, 8, 256, src, n + g_at)
                    else:
                        src = w_dn[bass.ds(g * 512, 512), (u - 8) * 512:(u - 7) * 512].rearrange(
                            "(k p) c -> p k c", p=P)
                        load(n, 4, 512, src, n + g_at)

            ffn_loads(None, w_up1, w_dn1, 0, 0)
            with nc.sync.Fori(1, GROUPS) as g:
                ffn_loads(FF1, w_up1, w_dn1, g, 12 * g - 12)
            for i in range(len(MIX_UNITS)):
                src, k, c = unit_src(i)
                load(MIX + i, k, c, src, MIX + i)
            with nc.sync.Fori(0, GROUPS) as g:
                ffn_loads(FF2, w_up2, w_dn2, g, 12 * g)
            for q in range(4):
                sp.wait_ge(out_ready, q + 1)
                sp.dma_start(out[:, 4 * q:4 * q + 4, :], X[:, 0, 4 * q:4 * q + 4, :]).then_inc(out_done, 16)
            sp.wait_ge(out_done, 64)

        BULK = (["lx0", "gt"] + [f"lx{p}" for p in range(1, 4)] + ["k0", "k1"] + [f"v{p}" for p in range(4)] + ["q0", "q1"]
                + [f"lg{p}" for p in range(4)] + ["o0", "o1"] + [f"woa{p}" for p in range(8)]
                + [f"wob{p}" for p in range(8)])
        EXTRA = {3: [("sel",)], 10: [("dec",)], 12: [("tr",)], 20: [("kt",)]}
        for b in range(LRU_N):
            EXTRA.setdefault(2 * b + 3, []).append(("gates", b))
        UPD = [(0, 0, 21), (1, 1, 22), (0, 1, 23), (1, 0, 24), (0, 2, 33), (1, 3, 34)]
        OUTS = [(0, 2, 0, 25), (0, 2, 1, 27), (1, 3, 0, 29), (1, 3, 1, 31),
                (0, 3, 0, 35), (0, 3, 1, 37), (1, 2, 0, 39), (1, 2, 1, 41)]
        for i, (d, c, t) in enumerate(UPD):
            EXTRA.setdefault(t, []).append(("upd", i))
        for i, (d, c, hh, t) in enumerate(OUTS):
            EXTRA.setdefault(t, []).append(("ds", i))
            EXTRA.setdefault(t + 1, []).append(("pv", i))
        EXTRA.setdefault(46, []).append(("ht",))
        ORDER = [e for t in sorted(EXTRA) for e in EXTRA[t]]
        EXT = {e: i for i, e in enumerate(ORDER)}

        def shift(i, s):
            return mod[:, s, 0, :] if i == 0 else modx[:, (3 if s else 1) if i == 1 else 6, :]

        def statistic(pe, mm, i, n):
            pe.wait_ge(sq_used, DT * (i + 1))
            mm(ps[:, 7, 0:n], c_("ones"), sqs[:, 0:n], start=True, stop=True).then_inc(stat_done, 1)

        def quarter_freed(eng, h0, q, g):
            eng.wait_ge(half_free[q % 2], h0[q % 2] + 2 + q // 2 + 3 * g)

        def bank_of(name):
            return 2 * (BULK.index(name) % 2)

        def unit_done(eng, *unit):
            eng.wait_ge(unit_used, MIX + TICK[unit] + 1)

        @block.tensor
        def _(pe):
            mm = nc.tensor.matmul

            def begin(n, more=0):
                pe.wait_ge(lo_done, splits(n) + more)

            def split_rows(k, n, bank, first, last_):
                for w, cond in ((WH, CH), (WL, CL)):
                    for q in range(4):
                        last = mm(ps[0:4, bank + q, :], cond[:, k, :], w[:, half_slot(n), q * 512:(q + 1) * 512],
                                  start=(first and w is WH), stop=(last_ and w is WL))
                last.then_inc(unit_used, 1)

            def columns(bank):
                for j in range(DT):
                    last = mm(ps[:, bank, 2 * j:2 * j + 2], rows4[0:4, j * P:(j + 1) * P], c_("comb")[0:4, :],
                              start=True, stop=True)
                last.then_inc(col_done, 1)

            pe.wait_ge(params_in, 32)
            pe.wait_ge(cond_ready, 1)
            for b in range(2):
                for p in range(DT // 2):
                    n = b * (DT // 2) + p
                    pe.wait_ge(early_full[n % 3], 16 * (n // 3 + 1))
                    for q in range(4):
                        mm(ps[0:4, q, :], CF[:, 2 * p + 1, :], early[:, n % 3, 1, q * 512:(q + 1) * 512],
                           start=(p == 0), stop=False)
                    begin(n)
                    split_rows(2 * p, n, 0, False, p == DT // 2 - 1)
                    if n == 9:
                        columns(4)
                    if n == 10:
                        statistic(pe, mm, 0, 512)
                if b == 0:
                    pe.wait_ge(half_free[0], 1)
            pe.wait_ge(cols_read, 1)
            pe.wait_ge(root_ready, 1)

            def products(bank, wh, wl, xh, xl, xhl, first, last, lat):
                o = ps[:, bank, :].rearrange("p (s t) -> p s t", s=2)
                if lat:
                    mm(o, wh, xhl, start=first, stop=False)
                    return mm(ps[:, bank, 0:SEQ], wl, xh, start=False, stop=last)
                mm(o, wh, xh, start=first, stop=False)
                mm(o, wh, xl, start=False, stop=False)
                return mm(o, wl, xh, start=False, stop=last)

            def ffn(base, h0, s0, g, lat, sums=False):
                ahead = g - 1 if base == FF1 else g
                for u in range(12):
                    if base is None:
                        n = AT0[u]
                        for a in (a for a in ATA if (AT0[u - 1] if u else 0) < a < n):
                            if a in UNSPLIT:
                                pe.wait_ge(stage_full[slot(a)], 16 * ((a - FIRST) // 3 + 1))
                                for q in range(4):
                                    last = mm(ps[0:4, 4 + q, :], CF[:, ATA.index(a), :],
                                              stage[:, slot(a), q * 512:(q + 1) * 512], start=False, stop=a == ATA[-1])
                                last.then_inc(unit_used, 1)
                                continue
                            begin(a)
                            split_rows(ATA.index(a), a, 4, a == ATA[0], a == ATA[-1])
                        if u == 0:
                            pe.wait_ge(half_free[0], 2)
                            columns(3)
                        if u == 2:
                            pe.wait_ge(cols_read, 2)
                        if u == 6:
                            pe.wait_ge(half_free[0], H_FF1[0] + 1)
                            columns(0)
                        if u == 8:
                            pe.wait_ge(cols_read, 3)
                    else:
                        n = base + u
                    if sums and u == 1:
                        pe.wait_ge(sums_done, 16 * g - 14)
                        for j in range(DT):
                            last = mm(ps[:, 3, j:j + 1], acc[:, j * P:(j + 1) * P], c_("ones", 0, 1), start=True, stop=True)
                        last.then_inc(late_cols, 1)
                    if sums and u == 2:
                        pe.wait_ge(late_read, g)
                    begin(n, 12 * ahead)
                    turn = u // 4 if u < 8 else u - 6
                    half = turn % 2
                    if u in (0, 4) or u >= 8:
                        pe.wait_ge(half_free[half], h0[half] + turn // 2 + 3 * g)
                    if u < 8:
                        w1, w2 = wv(WH, half_slot(n), 8, 256), wv(WL, half_slot(n), 8, 256)
                        for kk in range(8):
                            k = 8 * (u % 2) + kk
                            if u in (0, 1):
                                pe.wait_ge(xsplit, s0 + k + 1)
                            for ct in range(2):
                                a, z = w1[:, kk, ct * P:(ct + 1) * P], w2[:, kk, ct * P:(ct + 1) * P]
                                bank = 4 * half + 2 * ((u // 2) % 2) + ct
                                if lat:
                                    last = products(bank, a, z, XL2[:, 0, k, :], None, XL2[:, :, k, :],
                                                    k == 0, k == DT - 1, True)
                                else:
                                    last = products(bank, a, z, XHL[:, :, 0, k, :], XHL[:, :, 1, k, :], None,
                                                    k == 0, k == DT - 1, False)
                    else:
                        w1, w2 = wv(WH, half_slot(n), 4, 512), wv(WL, half_slot(n), 4, 512)
                        for j in range(4):
                            if u == 8:
                                pe.wait_ge(hid_ready, (4 * GROUPS if lat else 0) + 4 * g + j + 1)
                            for ct in range(4):
                                a, z = w1[:, j, ct * P:(ct + 1) * P], w2[:, j, ct * P:(ct + 1) * P]
                                if lat:
                                    last = products(4 * half + ct, a, z, HHL[:, 0, j, 0:SEQ], None,
                                                    HHL[:, :, j, 0:SEQ], j == 0, j == 3, True)
                                else:
                                    h1 = HHL[:, 0, j, :].rearrange("p (s t) -> p s t", s=2)
                                    h2 = HHL[:, 1, j, :].rearrange("p (s t) -> p s t", s=2)
                                    last = products(4 * half + ct, a, z, h1, h2, None, j == 0, j == 3, False)
                    last.then_inc(unit_used, 1)

            ffn(None, H_FF1, 0, 0, False)
            with nc.tensor.Fori(1, 10) as g:
                ffn(FF1, H_FF1, 0, g, False, True)
            ffn(FF1, H_FF1, 0, GROUPS - 1, False)

            pe.wait_ge(half_free[1], H_FF2[1])
            statistic(pe, mm, 1, 512)

            def extra(e):
                i = EXT[e]
                if i >= 1:
                    pe.wait_ge(ext_free, i)
                kind = e[0]
                if kind == "sel":
                    pe.wait_ge(bulk_free[1], 1)
                    for q in range(2):
                        last = mm(ps[0:40, 4 + q, :], c_("sel", 40 * q, 40 * q + 40)[0:32, :], GT, start=True, stop=True)
                elif kind == "gates":
                    b = e[1]
                    pe.wait_ge(conv_done, b + 1)
                    pe.wait_ge(lruw_in, 16 * (b + 1))
                    for q in range(4):
                        last = mm(ps[:, 4 + q, :], LW[:, q, :], xc[:, b % 2, :], start=True, stop=True)
                elif kind == "dec":
                    pe.wait_ge(dec_rhs, 1)
                    last = mm(ps[:, 4, 0:32], c_("parity")[0:40, :], mst[0:40, 16:48], start=True, stop=True)
                elif kind == "tr":
                    pe.wait_ge(exp_rows, 1)
                    src = ([rows[0:40, 0, (2 + c) * P:(3 + c) * P] for c in range(2)]
                           + [rows[0:40, 1, c * P:(c + 1) * P] for c in range(4)]
                           + [rows[0:40, 2, c * P:(c + 1) * P] for c in range(4)])
                    for q, r in enumerate(src):
                        last = nc.tensor.transpose(ps[:, 4, q * 40:(q + 1) * 40], r, c_("ident")[0:40, 0:40])
                elif kind == "kt":
                    for j in range(4):
                        for c in range(2):
                            last = nc.tensor.transpose(ps[:, 4 + j // 2, (j % 2) * 256 + c * P:(j % 2) * 256 + (c + 1) * P],
                                                       knat[:, 2 + c, j * P:(j + 1) * P], c_("ident"))
                elif kind == "upd":
                    d, c, _ = UPD[e[1]]
                    pe.wait_ge(kw_done, e[1] + 1)
                    for j in range(4):
                        last = mm(ps[:, 4 + j, 0:258].rearrange("p (a v) -> p a v", a=2), kw[:, j * P:(j + 1) * P],
                                  vaug[:, c, 2 * j:2 * j + 2, 0:129], start=True, stop=True)
                elif kind == "ds":
                    d, c, hh, _ = OUTS[e[1]]
                    if e[1] == 0:
                        for q in ("q0", "q1"):
                            pe.wait_ge(bulk_free[BULK.index(q) % 2], BULK.index(q) // 2 + 1)
                    for i4 in range(4):
                        h = 4 * hh + i4
                        mm(ps[:, 4, i4 * P:(i4 + 1) * P],
                           c_("ident")[0:40, 32 * d + h:32 * d + h + 1].to_broadcast([40, P]),
                           rows[0:40, 3, c * P:(c + 1) * P], start=True, stop=True)
                        last = mm(ps[:, 5, i4 * P:(i4 + 1) * P], kT[:, h // 2, (c - 2) * P:(c - 1) * P],
                                  qz[:, h % 2, h // 2, (c - 2) * P:(c - 1) * P], start=True, stop=True)
                elif kind == "pv":
                    d, c, hh, _ = OUTS[e[1]]
                    for i4 in range(4):
                        h = 4 * hh + i4
                        col = (i4 % 2) * 129
                        mm(ps[:, 4 + i4 // 2, col:col + 129], Dx[:, i4, :], vaug[:, c, h, 0:129], start=True, stop=True)
                        last = mm(ps[:, 6 + i4 // 2, col:col + 129], qz[:, h % 2, h // 2, (c - 2) * P:(c - 1) * P],
                                  C[:, d, h // 2, (h % 2) * 129:(h % 2) * 129 + 129], start=True, stop=True)
                elif kind == "ht":
                    pe.wait_ge(hn_done, 2)
                    for c in range(2):
                        for h in range(HEADS):
                            last = nc.tensor.transpose(ps[:, 4 + 2 * c + h // 4, (h % 4) * P:(h % 4 + 1) * P],
                                                       Hs[:, c, h, :], c_("ident"))
                last.then_inc(ext_done, 1)

            for i, (kind, p, h) in enumerate(MIX_UNITS):
                n = MIX + i
                begin(n)
                name = kind if kind == "gt" else f"{kind}{p}"
                t = BULK.index(name)
                bank = bank_of(name)
                if h == 0:
                    if t < 2:
                        pe.wait_ge(half_free[0], H_FF2[0])
                    else:
                        pe.wait_ge(bulk_free[t % 2], t // 2)
                s = half_slot(n)
                if kind == "gt":
                    for k in range(DT):
                        a, z = WH[:, s, k * 32:(k + 1) * 32], WL[:, s, k * 32:(k + 1) * 32]
                        o = ps[0:32, bank, :].rearrange("p (s t) -> p s t", s=2)
                        mm(o, a, XHL[:, :, 0, k, :], start=(k == 0), stop=False)
                        mm(o, a, XHL[:, :, 1, k, :], start=False, stop=False)
                        last = mm(o, z, XHL[:, :, 0, k, :], start=False, stop=(k == DT - 1))
                elif kind in ("lx", "lg", "q", "woa", "wob"):
                    w1, w2 = wv(WH, s, 8, 256), wv(WL, s, 8, 256)
                    if kind == "woa":
                        pe.wait_ge(mxa_done, 1)
                    if kind == "wob":
                        pe.wait_ge(mxb_done, 1)
                    for kk in range(8):
                        k = 8 * h + kk
                        if i < 2:
                            pe.wait_ge(xsplit, DT + k + 1)
                        for ct in range(2):
                            a, z = w1[:, kk, ct * P:(ct + 1) * P], w2[:, kk, ct * P:(ct + 1) * P]
                            if kind == "lx":
                                last = products(bank + ct, a, z, XHL[:, :, 0, k, :], XHL[:, :, 1, k, :], None,
                                                k == 0, k == DT - 1, False)
                            elif kind in ("lg", "q"):
                                last = products(bank + ct, a, z, XHL[:, 1, 0, k, :], None, XHL[:, 1, :, k, :],
                                                k == 0, k == DT - 1, True)
                            else:
                                m = MXA if kind == "woa" else MXB
                                last = products(bank + ct, a, z, m[:, 0, kk, :], None, m[:, :, kk, :],
                                                kk == 0, kk == 7, True)
                else:
                    nk, nw, toks = (4, 512, (2, 3)) if kind == "o" else (8, 256, range(4))
                    w1, w2 = wv(WH, s, nk, nw), wv(WL, s, nk, nw)
                    for kk in range(nk):
                        k = nk * h + kk
                        for ti, tt in enumerate(toks):
                            xh, xl = (XHL[:, tt // 2, q, k, (tt % 2) * P:(tt % 2 + 1) * P] for q in range(2))
                            if kind == "o":
                                o = ps[:, bank + ti, :]
                                fresh = True
                            else:
                                o = ps[:, bank + ti // 2, (ti % 2) * 256:(ti % 2 + 1) * 256]
                                fresh = ti % 2 == 0
                            shared = kind != "o"
                            mm(o, xh, w1[:, kk, :], start=(k == 0 and fresh), stop=False, skip_group_check=shared)
                            mm(o, xl, w1[:, kk, :], start=False, stop=False, skip_group_check=shared)
                            last = mm(o, xh, w2[:, kk, :], start=False, stop=(k == DT - 1), skip_group_check=shared)
                last.then_inc(unit_used, 1)
                for e in EXTRA.get(i, []):
                    extra(e)

            pe.wait_ge(ext_free, len(ORDER))
            statistic(pe, mm, 2, SEQ)
            for t in (0, 1):
                pe.wait_ge(bulk_free[t], (len(BULK) + 1 - t) // 2)
            with nc.tensor.Fori(0, GROUPS - 1) as g:
                ffn(FF2, H_FF2, 2 * DT, g, True)
            ffn(FF2, H_FF2, 2 * DT, GROUPS - 1, True)
            pe.wait_ge(half_free[1], H_FF2[1] + 3 * GROUPS)
            statistic(pe, mm, 3, SEQ)

        @block.scalar
        def _(act):
            A = nc.scalar.activation

            def split(n, g=0):
                if n < FIRST:
                    act.wait_ge(early_full[n % 3], 16 * (n // 3 + 1))
                    src = early[:, n % 3, 0, :]
                else:
                    act.wait_ge(stage_full[slot(n)], 16 * ((n - FIRST) // 3 + 1) + 64 * g)
                    src = stage[:, slot(n), :]
                if n >= 2:
                    act.wait_ge(unit_used, slot_before(n) + 1 + 12 * g)
                A(WH[:, half_slot(n), :], src, ACT.Copy).then_inc(hi_done, 1)

            def squares(i, d, lat):
                if DT * i + d >= 2:
                    act.wait_ge(sq_used, DT * i + d - 1)
                if not lat:
                    A(sq[:, d % 2, :].rearrange("p (s t) -> p s t", s=2), X[:, :, d, :], ACT.Square).then_inc(sq_done, 1)
                else:
                    A(sq[:, d % 2, 0:256], X[:, 1, d, :], ACT.Square).then_inc(sq_done, 1)

            def root(i, n):
                act.wait_ge(stat_done, i + 1)
                A(rms[:, 0:n], ps[:, 7, 0:n], ACT.Sqrt, scale=1.0 / D_MODEL, bias=c_("eps")).then_inc(root_ready, 1)

            def modulate(i, d, lat):
                act.wait_ge(xn_done, DT * i + d + 1)
                if i == 0 and d >= 2:
                    act.wait_ge(xsplit, d - 1)
                for s in ((1,) if lat else (0, 1)):
                    c = 0 if lat else 256 * s
                    if i == 0:
                        last = A(xm[:, d % 2, c:c + 256], xn1[:, s, d, :], ACT.Identity,
                                 bias=shift(i, s)[:, d:d + 1], scale=scl[:, i, s, d:d + 1])
                    else:
                        last = A(XL2[:, 0, d, :] if lat else XHL[:, s, 0, d, :], xn[:, d % 4, c:c + 256], ACT.Identity,
                                 bias=shift(i, s)[:, d:d + 1])
                last.then_inc(xm_done, 1)

            act.wait_ge(params_in, 32)
            A(silc[:], v_("c"), ACT.Silu).then_inc(cond_silu, 1)
            act.wait_ge(cond_silu, 1)
            sv = silc[:].rearrange("p (s k) -> p k s", s=2)
            A(CH[:, :, 0:4:2], sv, ACT.Copy)
            act.wait_ge(zeros_set, 1)
            A(CF[:, :, 0:4:2], sv, ACT.Copy)
            A(CL[:, :, 0:4:2], sv, ACT.Copy).then_inc(cond_silu, 1)
            act.wait_ge(rate_arg, 1)
            A(lsp[:, 1, :], lsp[:, 1, :], ACT.Exp, scale=-1.0).then_inc(rate_exp, 1)
            act.wait_ge(rate_u, 1)
            A(lsp[:, 0, :], lsp[:, 0, :], ACT.Ln).then_inc(rate_ln, 1)

            split(0)
            def rows_on_chip(b, n, bank):
                act.wait_ge(unit_used, n + 1)
                if b >= 1:
                    act.wait_ge(col_done, b)
                A(rows4[0:4, :].rearrange("p (q n) -> p q n", q=4), ps[0:4, bank:bank + 4, :], ACT.Copy).then_inc(
                    half_free[bank // 4], 1)

            for n in range(PAIRS):
                if n == DT // 2 - 1:
                    rows_on_chip(0, n, 0)
                split(n + 1)
                if n == 2:
                    act.wait_ge(x_in, 32)
                if 2 <= n < 10:
                    squares(0, 2 * n - 4, False)
                    squares(0, 2 * n - 3, False)
                if n == 11:
                    root(0, 512)
            rows_on_chip(1, PAIRS - 1, 0)
            split(PAIRS + 1)
            act.wait_ge(scl_ready, 1)
            for d in range(DT):
                modulate(0, d, False)
                if d in SPLIT_AFTER:
                    split(SPLIT_AFTER[d])

            def ada_loads(g, block, t):
                for k in ADA_TICKS.get(t, ()):
                    act.wait_ge(sums_done, 16 * g + k - 15)
                    act.dma_start(astage[:, k % 2, :], ada_w[k * P:(k + 1) * P, bass.ds(block * UW, UW)]).then_inc(
                        ada_full[k % 2], 16)

            def ffn(base, h0, g, lat, last_group=False, norm=None, block=None):
                e0 = 4 * GROUPS if lat else 0
                ahead = g - 1 if base == FF1 else g
                for u in range(12):
                    n = AT0[u] if base is None else base + u
                    if base is None:
                        for m in range(max(LAST_EARLY, AT0[u - 1] + 1 if u else 0), n + 1):
                            if m + 1 > LAST_EARLY and m + 1 not in UNSPLIT:
                                split(m + 1)
                        if u == 3:
                            rows_on_chip(2, ATA[-1], 4)
                    elif lat:
                        if u != 7 and not (last_group and u >= 10):
                            split(base + u + 2, ahead)
                    elif not (last_group and u == 11):
                        split(base + u + 1, ahead)
                    if block is not None:
                        ada_loads(g, block, u)
                    if norm is not None and u >= 9:
                        quarter_freed(act, h0, u - 9, g)
                        for d in range(4 * (u - 9), 4 * (u - 8)):
                            squares(norm, d, lat)
                    if u >= 8:
                        continue
                    half = u // 4
                    gate, up = 4 * half, 4 * half + 2
                    if u % 4 == 1:
                        act.wait_ge(unit_used, n + 1 + 12 * ahead)
                        if not lat:
                            if half == 1:
                                act.wait_ge(hid_ready, 4 * g + 2)
                            for ct in range(2):
                                A(G[:, ct, :], ps[:, gate + ct, :], ACT.Silu).then_inc(silu_done, 1)
                        else:
                            act.wait_ge(hid_ready, e0 + 4 * g + 2 * half)
                            A(U[:, :, 0:256], ps[:, gate:gate + 2, 256:512], ACT.Copy).then_inc(gate_lo, 1)
                            act.wait_ge(gate_sum, 2 * g + half + 1)
                            A(G[:, :, 0:256], G[:, :, 0:256], ACT.Silu).then_inc(silu_done, 1)
                    if u % 4 == 3:
                        if not lat:
                            for ct in range(2):
                                if ct == 0:
                                    act.wait_ge(prod_done, 2 * g + half + 1)
                                else:
                                    act.wait_ge(half_free[half], h0[half] + 3 * g + 1)
                                A(HHL[:, 0, 2 * half + ct, :], G[:, ct, :], ACT.Copy).then_inc(hid_hi, 1)
                        else:
                            act.wait_ge(unit_used, n + 1 + 12 * ahead)
                            for ct in range(2):
                                A(U[:, ct, 256:512], ps[:, up + ct, 256:512], ACT.Copy).then_inc(up_lo, 1)
                            for ct in range(2):
                                act.wait_ge(prod_done, 2 * GROUPS + 4 * g + 2 * half + ct + 1)
                                A(HHL[:, 0, 2 * half + ct, 0:256], G[:, ct, 0:256], ACT.Copy).then_inc(hid_hi, 1)
                    if lat and u == 7:
                        split(base + u + 2, ahead)

            ffn(None, H_FF1, 0, False)
            act.wait_ge(col_done, 3)
            act.wait_ge(xsplit, DT)
            with nc.scalar.Fori(1, 3) as g:
                ffn(FF1, H_FF1, g, False, block=g + 2)
            with nc.scalar.Fori(3, 9) as g:
                ffn(FF1, H_FF1, g, False, block=g)
            ffn(FF1, H_FF1, 9, False)
            ffn(FF1, H_FF1, GROUPS - 1, False, norm=1)

            for t in range(2):
                act.wait_ge(half_free[t], H_FF2[t])
            for d in range(12, DT):
                squares(1, d, False)
            root(1, 512)
            for d in range(DT):
                modulate(1, d, False)
                if d == 5:
                    split(MIX + 1)

            def extra_ready(*e):
                act.wait_ge(ext_done, EXT[e] + 1)

            def load_lru(b):
                act.dma_start(LW, lru_w[:, b]).then_inc(lruw_in, 16)

            def tick(i):
                def turn_done(name, *unit):
                    unit_done(act, *unit)
                    return bank_of(name), bulk_free[BULK.index(name) % 2]

                if i == 0:
                    act.wait_ge(xsplit, 2 * DT)
                    load_lru(0)
                if i == 2:
                    bk, free = turn_done("gt", "gt", 0, 0)
                    A(GT, ps[0:32, bk, :], ACT.Copy).then_inc(free, 1)
                if 3 <= i <= 19:
                    b, phase = divmod(i - 3, 2)
                    if phase == 1 and b < LRU_N:
                        extra_ready("gates", b)
                        if b < LRU_N - 1:
                            load_lru(b + 1)
                        if b >= 1:
                            act.wait_ge(lru_done, b)
                        for d in range(2):
                            A(Rg[:, d, :], ps[:, 4 + 2 * d, :], ACT.Sigmoid, bias=v_("b_r", d * 8 + b, d * 8 + b + 1))
                            A(Ig[:, d, :], ps[:, 5 + 2 * d, :], ACT.Sigmoid,
                              bias=v_("b_i", d * 8 + b, d * 8 + b + 1)).then_inc(act_step, 1)
                        act.wait_ge(act_step, 2 + 2 * (b + 1) + b * 2)
                        for d in range(2):
                            A(Ag[:, d, :], Rg[:, d, :], ACT.Exp, scale=lsp[:, 0, d * 8 + b:d * 8 + b + 1])
                            A(Rg[:, d, :], Rg[:, d, :], ACT.Tanh,
                              scale=lsp[:, 1, d * 8 + b:d * 8 + b + 1]).then_inc(act_step, 1)
                        act.wait_ge(act_step, 2 + 4 * (b + 1))
                        A(ps[:, 4:6, :], Ag, ACT.Square).then_inc(act_a, 1)
                    elif phase == 0:
                        if b < LRU_N:
                            if b % 2 == 0:
                                act.wait_ge(bulk_free[BULK.index(f"lx{b // 2}") % 2], BULK.index(f"lx{b // 2}") // 2 + 1)
                            if b >= 2:
                                act.wait_ge(lru_done, b - 1)
                            if b == 0:
                                act.wait_ge(pads_set, 1)
                            if b == 1:
                                act.wait_ge(ext_done, EXT[("sel",)] + 1)
                            A(xc[:, b % 2, :].rearrange("p (s t) -> p s t", s=2), xpad[:, b, :, 0:256], ACT.Identity,
                              bias=v_("conv_b", b, b + 1), scale=v_("conv_w", b, b + 1)).then_inc(conv_first, 1)
                        if b >= 1:
                            act.wait_ge(z_done, b)
                            A(Rg, Rg, ACT.Sqrt).then_inc(root_z, 1)
                if i == 3:
                    extra_ready("sel")
                    A(rows[0:40, 0, :], ps[0:40, 4, :], ACT.Identity, bias=v_("mg", 0, 1)[0:40, :])
                    A(rows[0:40, 1, :], ps[0:40, 5, :], ACT.Identity, bias=v_("mg", 1, 2)[0:40, :]).then_inc(ext_free, 1)
                    act.wait_ge(ext_free, EXT[("sel",)] + 1)
                    A(rows[0:40, 2, :], rows[0:40, 1, :], ACT.Abs).then_inc(act_step, 1)
                    act.wait_ge(act_step, 1)
                    A(rows[0:40, 2, :], rows[0:40, 2, :], ACT.Exp, scale=-1.0).then_inc(act_step, 1)
                    act.wait_ge(act_step, 2)
                    A(rows[0:40, 2, :], rows[0:40, 2, :], ACT.Ln, bias=c_("one")[0:40, :]).then_inc(log_done, 1)
                if i in (2, 4, 6, 8):
                    p = i // 2 - 1
                    bk, free = turn_done(f"lx{p}", "lx", p, 1)
                    A(xpad[:, 2 * p:2 * p + 2, 0, 2:258], ps[:, bk:bk + 2, 0:256], ACT.Copy)
                    for a in range(2):
                        last = A(xpad[:, 2 * p + a, 1, 2:258].rearrange("p (r c) -> p c r", r=ROWS),
                                 ps[:, bk + a, 256:512].rearrange("p (c r) -> p c r", r=ROWS), ACT.Copy)
                    last.then_inc(free, 1)
                if i == 7:
                    act.wait_ge(enm_arg, 1)
                    for c in (2, 3):
                        A(rows[0:40, 1, (c - 2) * P:(c - 1) * P], rows[0:40, 3, c * P:(c + 1) * P], ACT.Exp,
                          scale=-1.0, bias=mst[0:40, c:c + 1])
                    A(rows[0:40, 1, 256:512], rows[0:40, 1, 256:512], ACT.Exp, scale=-1.0)
                    for c in range(4):
                        A(rows[0:40, 2, c * P:(c + 1) * P], rows[0:40, 0, c * P:(c + 1) * P], ACT.Exp,
                          bias=mst[0:40, 4 + c:5 + c])
                    A(mst[0:40, 8:12], mst[0:40, 8:12], ACT.Exp).then_inc(exp_rows, 1)
                if i in (10, 12):
                    p = (i - 10) // 2
                    bk, free = turn_done(f"k{p}", "k", p, 1)
                    A(knat[:, :, p * 256:(p + 1) * 256],
                      ps[:, bk:bk + 2, :].rearrange("p b (a n) -> p (b a) n", a=2), ACT.Copy,
                      scale=DK ** -0.5).then_inc(free, 1)
                if i in (14, 16, 18, 20):
                    p = (i - 14) // 2
                    bk, free = turn_done(f"v{p}", "v", p, 1)
                    for b2 in range(2):
                        last = A(vaug[:, 2 * b2:2 * b2 + 2, 2 * p:2 * p + 2, 0:DV],
                                 ps[:, bk + b2, :].rearrange("p (a h v) -> p a h v", a=2, h=2), ACT.Copy)
                    last.then_inc(free, 1)
                if i in (22, 24):
                    p = (i - 22) // 2
                    bk, free = turn_done(f"q{p}", "q", p, 1)
                    if p == 1:
                        act.wait_ge(bulk_free[BULK.index("q0") % 2], BULK.index("q0") // 2 + 1)
                    A(Dx[:, 0:2, :].rearrange("p a t -> p (a t)"), ps[:, bk, 256:512], ACT.Copy)
                    A(Dx[:, 2:4, :].rearrange("p a t -> p (a t)"), ps[:, bk + 1, 256:512], ACT.Copy).then_inc(lo_copy, 1)
                for j, (d, c, hh, t) in enumerate(OUTS):
                    if i == t + 1:
                        act.wait_ge(d_masked, j + 1)
                        for i4 in range(4):
                            h = 32 * d + 4 * hh + i4
                            last = A(Dx[:, i4, :], Dx[:, i4, :], ACT.Exp, bias=tr[:, c - 2, h:h + 1])
                        last.then_inc(d_exp, 1)
                    if i == t + 2:
                        extra_ready("pv", j)
                        if j >= 1:
                            act.wait_ge(num_done, j)
                        for i4 in range(4):
                            h = 32 * d + 4 * hh + i4
                            last = A(t1[:, i4, :], ps[:, 6 + i4 // 2, (i4 % 2) * 129:(i4 % 2) * 129 + 129], ACT.Copy,
                                     scale=tr[:, c, h:h + 1])
                        last.then_inc(inter_done, 1)
                if i in (26, 28, 30, 32):
                    p = (i - 26) // 2
                    bk, free = turn_done(f"lg{p}", "lg", p, 1)
                    if p == 0:
                        act.wait_ge(lru_done, LRU_N)
                    A(lgs[:, 2 * p:2 * p + 2, :], ps[:, bk:bk + 2, 256:512], ACT.Copy).then_inc(lo_copy, 1)
                if i == 34:
                    for q in ("lg2", "lg3"):
                        act.wait_ge(bulk_free[BULK.index(q) % 2], BULK.index(q) // 2 + 1)
                    A(lgs, lgs, ACT.Gelu_apprx_tanh).then_inc(gelu_done, 1)
                if i == 36:
                    act.wait_ge(lru_mul, 1)
                    A(MXA[:, 0], lgs, ACT.Copy).then_inc(mxa_hi, 1)
                if i in (36, 40):
                    p = (i - 36) // 4
                    bk, free = turn_done(f"o{p}", "o", p, 3)
                    A(SO[:, :, p * 512:(p + 1) * 512], ps[:, bk:bk + 2, :], ACT.Sigmoid).then_inc(free, 1)
                if i in (41, 44):
                    c = 1 if i == 41 else 0
                    act.wait_ge(hms, 1 + (i == 44))
                    A(mst[:, 48 + 8 * c:56 + 8 * c], mst[:, 48 + 8 * c:56 + 8 * c], ACT.Sqrt, scale=1.0 / DV,
                      bias=c_("eps")).then_inc(hroot, 1)
                if i == 47:
                    act.wait_ge(ext_free, EXT[("ht",)] + 1)
                    A(MXB[:, 0], Hs[:, :, :, :].rearrange("p c h v -> p (c h v)").rearrange("p (h t) -> p h t", h=8),
                      ACT.Copy).then_inc(mxb_hi, 1)

            for i in range(len(MIX_UNITS)):
                if i >= 1:
                    split(MIX + i + 1)
                tick(i)
                if i >= 50:
                    p = i - 50
                    act.wait_ge(bulk_free[BULK.index(f"wob{p}") % 2], BULK.index(f"wob{p}") // 2 + 1)
                    squares(2, 2 * p, True)
                    squares(2, 2 * p + 1, True)

            split(FF2 + 1)
            for t in (0, 1):
                act.wait_ge(bulk_free[t], (len(BULK) + 1 - t) // 2)
            for d in (14, 15):
                squares(2, d, True)
            root(2, SEQ)
            for d in range(DT):
                modulate(2, d, True)
            with nc.scalar.Fori(0, GROUPS - 1) as g:
                ffn(FF2, H_FF2, g, True)
            ffn(FF2, H_FF2, GROUPS - 1, True, last_group=True, norm=3)
            for t in range(2):
                act.wait_ge(half_free[t], H_FF2[t] + 3 * GROUPS)
            for d in range(12, DT):
                squares(3, d, True)
            root(3, SEQ)

        @block.gpsimd
        def _(pool):
            unit_done(pool, "v", 3, 1)
            nc.gpsimd.memset(qz[0:64, 1], 0.0)
            nc.gpsimd.memset(qz[64:128, 0], 0.0).then_inc(qz_zero, 1)
            pool.wait_ge(mxa_done, 1)
            pool.wait_ge(hn_done, 2)
            nc.gpsimd.memset(X[:, 0, :, :], 0.0).then_inc(sum_zero, 1)

        @block.vector
        def _(dve):
            TT, TS, STT = nc.vector.tensor_tensor, nc.vector.tensor_scalar, nc.vector.scalar_tensor_tensor
            steps = [0]

            def link(ins):
                steps[0] += 1
                ins.then_inc(dve_step, 1)
                dve.wait_ge(dve_step, steps[0])

            def split(n, g=0):
                dve.wait_ge(hi_done, splits(n) + 12 * g)
                src = early[:, n % 3, 0, :] if n < FIRST else stage[:, slot(n), :]
                TT(WL[:, half_slot(n), :], src, WH[:, half_slot(n), :].bitcast(F),
                   ALU.subtract).then_inc(lo_done, 1)

            def add_squares(i, d0, d1, n):
                for d in range(d0, d1):
                    dve.wait_ge(sq_done, DT * i + d + 1)
                    if d == 0:
                        nc.vector.tensor_copy(sqs[:, 0:n], sq[:, 0, 0:n]).then_inc(sq_used, 1)
                    else:
                        dve.wait_ge(sq_used, DT * i + d)
                        TT(sqs[:, 0:n], sqs[:, 0:n], sq[:, d % 2, 0:n], ALU.add).then_inc(sq_used, 1)

            def inverse(i, n):
                dve.wait_ge(root_ready, i + 1)
                nc.vector.reciprocal(rms[:, 0:n], rms[:, 0:n]).then_inc(rms_ready, 1)
                dve.wait_ge(rms_ready, i + 1)

            def normed(i, d, lat):
                if i == 0:
                    last = TT(xn1[:, :, d, :], X[:, :, d, :], rms[:].rearrange("p (s t) -> p s t", s=2), ALU.mult)
                else:
                    if d >= 4:
                        dve.wait_ge(xsplit, DT * i + d - 3)
                    for s in ((1,) if lat else (0, 1)):
                        c = 0 if lat else 256 * s
                        last = STT(xn[:, d % 4, c:c + 256], X[:, s, d, :], scl[:, i, s, d:d + 1], rms[:, c:c + 256],
                                   ALU.mult, ALU.mult)
                last.then_inc(xn_done, 1)

            def x_split(i, d, lat):
                dve.wait_ge(xm_done, DT * i + d + 1)
                if i == 0:
                    src = xm[:, d % 2, :].rearrange("p (s t) -> p s t", s=2)
                    h = XHL[:, :, 0, d, :]
                    link(nc.vector.tensor_copy(h, src))
                    last = TT(XHL[:, :, 1, d, :], src, h.bitcast(F), ALU.subtract)
                else:
                    for s in ((1,) if lat else (0, 1)):
                        c = 0 if lat else 256 * s
                        h = XL2[:, 0, d, :] if lat else XHL[:, s, 0, d, :]
                        l = XL2[:, 1, d, :] if lat else XHL[:, s, 1, d, :]
                        last = STT(l, xn[:, d % 4, c:c + 256], shift(i, s)[:, d:d + 1], h.bitcast(F),
                                   ALU.add, ALU.subtract)
                last.then_inc(xsplit, 1)

            def norm_tiles(i, lat, split_at=None):
                for d in range(DT + 2):
                    if d < DT:
                        normed(i, d, lat)
                    if d >= 2:
                        x_split(i, d - 2, lat)
                    if d == split_at:
                        split(MIX + 1)

            dve.wait_ge(params_in, 32)
            nc.vector.memset(zer[:], 0.0)
            nc.vector.memset(CF[:], 0.0)
            nc.vector.memset(CL[:].bitcast(mybir.dt.uint32), 0).then_inc(zeros_set, 1)
            STT(lsp[:, 1, :], v_("lam"), -1.0, v_("lam"), ALU.mult, ALU.max).then_inc(rate_arg, 1)
            dve.wait_ge(cond_silu, 2)
            sv = silc[:].rearrange("p (s k) -> p k s", s=2)
            TT(CH[:, :, 1:4:2], sv, CH[:, :, 0:4:2].bitcast(F), ALU.subtract).then_inc(cond_ready, 1)

            e_, l_ = lsp[:, 1, :], lsp[:, 0, :]
            u_, z_, m_ = (rate[:, q, :] for q in range(3))
            dve.wait_ge(rate_exp, 1)
            link(TS(u_, e_, 1.0, None, ALU.add))
            link(nc.vector.tensor_copy(l_, u_))
            link(TS(u_, u_, -1.0, None, ALU.add))
            TS(z_, u_, 0.0, None, ALU.is_equal)
            TS(u_, u_, 1e-30, None, ALU.max).then_inc(rate_u, 1)
            dve.wait_ge(rate_u, 1)
            link(nc.vector.reciprocal(u_, u_))
            link(TT(z_, z_, e_, ALU.mult))
            link(TT(u_, u_, e_, ALU.mult))
            dve.wait_ge(rate_ln, 1)
            link(TT(l_, l_, u_, ALU.mult))
            TS(m_, v_("lam"), -1.0, 0.0, ALU.mult, ALU.max)
            link(TT(l_, l_, z_, ALU.add))
            link(TT(l_, l_, m_, ALU.add))
            link(TS(lsp[:, 1, :], l_, 8.0, None, ALU.mult))
            link(TS(lsp[:, 0, :], l_, -8.0, None, ALU.mult))

            split(0)
            def mod_columns(b, bank):
                dve.wait_ge(col_done, b + 1)
                TT(mod[:, :, b, :], ps[:, bank, 0:32].rearrange("p (j s) -> p s j", s=2),
                   v_("ada_b", b * DT, (b + 1) * DT).rearrange("p (s j) -> p s j", s=1).to_broadcast([P, 2, DT]),
                   ALU.add).then_inc(cols_read, 1)
                dve.wait_ge(cols_read, b + 1)
                if b == 1:
                    for s in range(2):
                        last = STT(scl[:, 0, s, :], mod[:, s, 1, :], 1.0, v_("n1"), ALU.add, ALU.mult)
                    last.then_inc(scl_ready, 1)
                if b == 2:
                    link(TS(hgate[:, 0], mod[:, :, 2, :], 0.5, None, ALU.mult))

            for n in range(PAIRS):
                split(n + 1)
                if 2 <= n < 10:
                    add_squares(0, 2 * n - 4, 2 * n - 2, 512)
                if n == 10:
                    mod_columns(0, 4)
                if n == 11:
                    inverse(0, 512)
                if n >= 12:
                    for d in range(4 * (n - 12), 4 * (n - 11)):
                        normed(0, d, False)
            split(PAIRS + 1)
            mod_columns(1, 3)
            for d in range(DT):
                x_split(0, d, False)
                if d in SPLIT_AFTER:
                    split(SPLIT_AFTER[d])

            def late_columns(g):
                dve.wait_ge(late_cols, g)
                at = bass.ds(g - 1, 1)
                TT(modx[:, at, :], ps[:, 3:4, 0:DT], v_("ada_bx").rearrange("p (q n) -> p q n", q=9)[:, at, :],
                   ALU.add).then_inc(late_read, 1)

            def ada_sums(g, s, u):
                for k in ADA_TICKS.get(u, ()):
                    c = silc[:, s * DT + k:s * DT + k + 1]
                    dve.wait_ge(ada_full[k % 2], 16 * (k // 2 + 1) + 128 * g - 128)
                    dve.wait_ge(sums_done, 16 * g + k - 14)
                    if k == 0:
                        dve.wait_ge(late_cols, g)
                        TS(acc[:], astage[:, 0, :], c, None, ALU.mult).then_inc(sums_done, 1)
                    else:
                        STT(acc[:], astage[:, k % 2, :], c, acc[:], ALU.mult, ALU.add).then_inc(sums_done, 1)

            def ffn(base, h0, gi, g, lat, last_group=False, columns=False, sums=None, norm=None):
                ahead = g - 1 if base == FF1 else g
                for u in range(12):
                    if u >= 1 and sums is not None:
                        ada_sums(g, sums, u - 1)
                    more = not (last_group and u + 1 + lat >= 12)
                    if base is None:
                        for m in range(max(LAST_EARLY, AT0[u - 1] + 1 if u else 0), AT0[u] + 1):
                            if m + 1 > LAST_EARLY and m + 1 not in UNSPLIT:
                                split(m + 1)
                        if u == 7:
                            mod_columns(2, 0)
                    elif more and not (lat and u in (7, 8, 9, 10)):
                        split(base + u + 1 + lat, ahead)
                    n_at = (AT0[u] if base is None else base + u) + 1 + 12 * ahead
                    if columns and u == 0:
                        late_columns(g)
                    half = u // 4
                    gate, up = 4 * half, 4 * half + 2
                    if u % 4 == 1 and u < 8 and lat:
                        dve.wait_ge(gate_lo, 2 * g + half + 1)
                        TT(G[:, :, 0:256], ps[:, gate:gate + 2, 0:256], U[:, :, 0:256], ALU.add).then_inc(gate_sum, 1)
                    if u % 4 == 3 and u < 8:
                        if not lat:
                            dve.wait_ge(unit_used, n_at)
                            for ct in range(2):
                                dve.wait_ge(silu_done, 4 * g + 2 * half + ct + 1)
                                TT(G[:, ct, :], ps[:, up + ct, :], G[:, ct, :], ALU.mult).then_inc(
                                    half_free[half] if ct else prod_done, 1)
                            for ct in range(2):
                                dve.wait_ge(hid_hi, 4 * g + 2 * half + ct + 1)
                                j = 2 * half + ct
                                TT(HHL[:, 1, j, :], G[:, ct, :], HHL[:, 0, j, :].bitcast(F),
                                   ALU.subtract).then_inc(hid_ready, 1)
                        else:
                            for ct in range(2):
                                dve.wait_ge(up_lo, 4 * g + 2 * half + ct + 1)
                                last = TT(U[:, ct, 256:512], ps[:, up + ct, 0:256], U[:, ct, 256:512], ALU.add)
                            last.then_inc(half_free[half], 1)
                            dve.wait_ge(half_free[half], h0[half] + 3 * g + 1)
                            dve.wait_ge(silu_done, 4 * GROUPS + 2 * g + half + 1)
                            for ct in range(2):
                                TT(G[:, ct, 0:256], G[:, ct, 0:256], U[:, ct, 256:512], ALU.mult).then_inc(prod_done, 1)
                            for ct in range(2):
                                j = 2 * half + ct
                                dve.wait_ge(hid_hi, 4 * GROUPS + 4 * g + j + 1)
                                dve.wait_ge(prod_done, 2 * GROUPS + 4 * g + j + 1)
                                TT(HHL[:, 1, j, 0:256], G[:, ct, 0:256], HHL[:, 0, j, 0:256].bitcast(F),
                                   ALU.subtract).then_inc(hid_ready, 1)
                    if lat and last_group and u < 8:
                        for d in (2 * u, 2 * u + 1):
                            last = STT(X[:, 1, d, :], X[:, 0, d, :], hgate[:, gi, 1, d:d + 1], X[:, 1, d, :],
                                       ALU.mult, ALU.add)
                        if u == 7:
                            link(last)
                    if norm is not None and u >= 9:
                        add_squares(norm, 4 * (u - 9), 4 * (u - 8), SEQ if lat else 512)
                    if u >= 8:
                        dve.wait_ge(unit_used, n_at)
                        half = u % 2
                        d0 = 4 * (u - 8)
                        if lat and not last_group:
                            for part in range(2):
                                last = TT(X[:, 0, d0:d0 + 4, :], X[:, 0, d0:d0 + 4, :],
                                          ps[:, 4 * half:4 * half + 4, part * 256:(part + 1) * 256], ALU.add)
                                if part == 0:
                                    last.then_inc(add_first, 1)
                                    dve.wait_ge(add_first, 4 * g + u - 7)
                        for part in (() if lat and not last_group else range(2)):
                            for ct in range(4):
                                d = 4 * (u - 8) + ct
                                s = 1 if lat else part
                                last = STT(X[:, s, d, :], ps[:, 4 * half + ct, part * 256:(part + 1) * 256],
                                           hgate[:, gi, s, d:d + 1], X[:, s, d, :], ALU.mult, ALU.add)
                                if lat and part == 0 and ct == 3:
                                    last.then_inc(add_first, 1)
                                    dve.wait_ge(add_first, 4 * g + u - 7)
                        last.then_inc(half_free[half], 1)
                    if more and lat and u in (7, 8, 9, 10):
                        split(base + u + 2, ahead)

            ffn(None, H_FF1, 0, 0, False)
            nc.vector.memset(acc[:], 0.0).then_inc(sums_done, 2)
            with nc.vector.Fori(1, 3) as g:
                ffn(FF1, H_FF1, 0, g, False, columns=True, sums=0)
            with nc.vector.Fori(3, 9) as g:
                ffn(FF1, H_FF1, 0, g, False, columns=True, sums=1)
            ffn(FF1, H_FF1, 0, 9, False, columns=True)
            ffn(FF1, H_FF1, 0, GROUPS - 1, False, norm=1)
            STT(scl[:, 1, 0, :], modx[:, 2, :], 1.0, v_("n2"), ALU.add, ALU.mult)
            STT(scl[:, 1, 1, :], modx[:, 4, :], 1.0, v_("n2"), ALU.add, ALU.mult)
            STT(scl[:, 2, 1, :], modx[:, 7, :], 1.0, v_("n3"), ALU.add, ALU.mult)
            link(TS(hgate[:, 1, 1, :], modx[:, 8, :], 0.5, None, ALU.mult))

            add_squares(1, 12, DT, 512)
            inverse(1, 512)
            norm_tiles(1, False, split_at=8)

            def extra_ready(*e):
                dve.wait_ge(ext_done, EXT[e] + 1)

            DIRS = [(0, 0, [0, 1, 2, 3]), (1, 32, [1, 0, 3, 2])]

            def ordered(row, q, c, d):
                v = rows[row:row + 8, q, c * P:(c + 1) * P]
                return v[:, ::-1] if d else v

            def tick(i):
                if i == 0:
                    dve.wait_ge(xsplit, 2 * DT)
                    nc.vector.memset(xpad[:, :, :, 0:2], 0.0)
                    nc.vector.memset(xpad[:, :, :, 258:260], 0.0).then_inc(pads_set, 1)
                    nc.vector.memset(vaug[:, :, :, DV:VS], 1.0)
                    nc.vector.memset(mst[:], 0.0)
                    link(nc.vector.memset(rows[:, 3, :], 0.0))
                if i == 4:
                    dve.wait_ge(log_done, 1)
                    link(STT(rows[0:40, 1, :], rows[0:40, 1, :], 0.0, rows[0:40, 2, :], ALU.min, ALU.subtract))
                    for d, r, order in DIRS:
                        for c in order:
                            last = nc.vector.tensor_tensor_scan(ordered(r, 2, c, d), ordered(r, 1, c, d), zer[r:r + 8, :],
                                                                0.0, ALU.add, ALU.add)
                    link(last)
                    link(TT(rows[0:40, 0, :], rows[0:40, 0, :], rows[0:40, 2, :], ALU.subtract))
                if i == 5:
                    for t in range(4):
                        for d, r, order in DIRS:
                            c = order[t]
                            last = nc.vector.tensor_tensor_scan(ordered(r, 3, c, d), ordered(r, 0, c, d), ordered(r, 0, c, d),
                                                                mst[r:r + 8, c:c + 1], ALU.max, ALU.max)
                        link(last)
                        if t < 3:
                            for d, r, order in DIRS:
                                e = order[t] * P + (0 if d else P - 1)
                                nxt = order[t + 1]
                                last = TT(mst[r:r + 8, nxt:nxt + 1], rows[r:r + 8, 2, e:e + 1],
                                          rows[r:r + 8, 3, e:e + 1], ALU.add)
                            link(last)
                if i == 6:
                    for d, r, _ in DIRS:
                        m = rows[r:r + 8, 3, :].rearrange("p (c t) -> p c t", c=4)[:, :, (0 if d else P - 1)]
                        last = TS(mst[r:r + 8, 4:8], m, -1.0, None, ALU.mult)
                    link(last)
                    TT(mst[0:40, 8:12], mst[0:40, 0:4], mst[0:40, 4:8], ALU.add)
                    TT(rows[0:40, 1, 256:512], rows[0:40, 2, 256:512], rows[0:40, 3, 256:512],
                       ALU.add).then_inc(enm_arg, 1)
                if i == 8:
                    dve.wait_ge(exp_rows, 1)
                    TT(mst[0:40, 16:48].rearrange("p (d c j) -> p d c j", d=2, c=4),
                       c_("jj")[0:40, :].rearrange("p (d c j) -> p d c j", d=2, c=4),
                       mst[0:40, 8:12].rearrange("p (d c j) -> p d c j", d=1, j=1).to_broadcast([40, 2, 4, 4]),
                       ALU.mult).then_inc(dec_rhs, 1)
                if i == 11:
                    extra_ready("dec")
                    nc.vector.tensor_copy(dec, ps[:, 4, 0:32]).then_inc(ext_free, 1)
                if i == 13:
                    extra_ready("tr")
                    nc.vector.tensor_copy(tr, ps[:, 4, 0:400].rearrange("p (q n) -> p q n", q=10)).then_inc(ext_free, 1)
                    dve.wait_ge(ext_free, EXT[("tr",)] + 1)
                if 3 <= i <= 19:
                    b, phase = divmod(i - 3, 2)
                    if phase == 0:
                        if b < LRU_N:
                            dve.wait_ge(conv_first, b + 1)
                            v = xc[:, b % 2, :].rearrange("p (s t) -> p s t", s=2)
                            for k in range(1, 4):
                                ins = STT(v, xpad[:, b, :, k:k + 256], v_("conv_w", k * 8 + b, k * 8 + b + 1), v,
                                          ALU.mult, ALU.add)
                                if k < 3:
                                    link(ins)
                            ins.then_inc(conv_done, 1)
                        if b >= 1:
                            bb = b - 1
                            dve.wait_ge(root_z, b)
                            link(TT(Ig, Ig, Rg, ALU.mult))
                            nc.vector.tensor_tensor_scan(Rg[:, 0, :], Ag[:, 0, :], Ig[:, 0, :], 0.0, ALU.mult, ALU.add)
                            link(nc.vector.tensor_tensor_scan(
                                Rg[:, 1, 0:256][:, ::-1], Ag[:, 1, 0:256][:, ::-1], Ig[:, 1, 0:256][:, ::-1],
                                0.0, ALU.mult, ALU.add))
                            link(nc.vector.tensor_tensor_scan(
                                Rg[:, 1, 256:512][:, ::-1], Ag[:, 1, 256:512][:, ::-1], Ig[:, 1, 256:512][:, ::-1],
                                Rg[:, 1, 0:1], ALU.mult, ALU.add))
                            TT(LO[:, bb, :], Rg[:, 0, 256:512], Rg[:, 1, 256:512], ALU.add).then_inc(lru_done, 1)
                    elif b < LRU_N:
                        dve.wait_ge(act_a, b + 1)
                        STT(Rg, ps[:, 4:6, :], 1.0, Rg, ALU.add, ALU.mult).then_inc(ext_free, 1)
                        TT(Ig, Ig, xc[:, b % 2:b % 2 + 1, :].to_broadcast([P, 2, 512]), ALU.mult).then_inc(z_done, 1)
                if i == 21:
                    extra_ready("kt")
                    nc.vector.tensor_copy(kT, ps[:, 4:6, :].rearrange("p b (j t) -> p (b j) t", j=2)).then_inc(ext_free, 1)
                for j, (d, c, t) in enumerate(UPD):
                    if i == t + 1:
                        extra_ready("upd", j)
                        first = c == (1 if d else 0)
                        if first:
                            nc.vector.tensor_copy(C[:, d], ps[:, 4:8, 0:258]).then_inc(ext_free, 1)
                        else:
                            for jj in range(4):
                                e = d * 16 + c * 4 + jj
                                last = STT(C[:, d, jj, :], C[:, d, jj, :], dec[:, e:e + 1], ps[:, 4 + jj, 0:258],
                                           ALU.mult, ALU.add)
                            last.then_inc(ext_free, 1)
                        dve.wait_ge(ext_free, EXT[("upd", j)] + 1)
                for j, (d, c, t) in enumerate(UPD):
                    if i == t:
                        TT(kw.rearrange("p (h n) -> p h n", h=8), knat[:, c, :].rearrange("p (h n) -> p h n", h=8),
                           tr[:, 6 + c, 32 * d:32 * d + 8].rearrange("p (h n) -> p h n", n=1).to_broadcast([P, 8, 64]),
                           ALU.mult).then_inc(kw_done, 1)
                if i in (22, 24):
                    p = (i - 22) // 2
                    bk = bank_of(f"q{p}")
                    dve.wait_ge(lo_copy, p + 1)
                    if p == 0:
                        dve.wait_ge(qz_zero, 1)
                    src = ps[:, bk:bk + 2, 0:256]
                    lo = Dx.rearrange("p a t -> p (a t)").rearrange("p (a t) -> p a t", a=2)
                    TT(qz[0:64, 0, 2 * p:2 * p + 2, :], src[0:64], lo[0:64], ALU.add)
                    TT(qz[64:128, 1, 2 * p:2 * p + 2, :], src[64:128], lo[64:128], ALU.add).then_inc(
                        bulk_free[BULK.index(f"q{p}") % 2], 1)
                for j, (d, c, hh, t) in enumerate(OUTS):
                    if i == t + 1:
                        extra_ready("ds", j)
                        msk = c_("maskb" if d else "maskf").rearrange("p (h t) -> p h t", h=1).to_broadcast([P, 4, P])
                        TT(Dx, msk, ps[:, 4, :].rearrange("p (h t) -> p h t", h=4), ALU.subtract).then_inc(d_masked, 1)
                        dve.wait_ge(d_exp, j + 1)
                        TT(Dx, Dx, ps[:, 5, :].rearrange("p (h t) -> p h t", h=4), ALU.mult).then_inc(ext_free, 1)
                    if i == t + 2:
                        dve.wait_ge(inter_done, j + 1)
                        tv = t1.rearrange("p (b i) v -> p b (i v)", b=2)
                        TT(tv, tv, ps[:, 4:6, 0:258], ALU.add).then_inc(ext_free, 1)
                        dve.wait_ge(ext_free, EXT[("pv", j)] + 1)
                        dn = mst[:, 64:68]
                        link(STT(dn, t1[:, :, 128], -1.0, t1[:, :, 128], ALU.mult, ALU.max))
                        link(TT(dn, dn, tr[:, 2 + c, 32 * d + 4 * hh:32 * d + 4 * hh + 4], ALU.max))
                        link(nc.vector.reciprocal(dn, dn))
                        db = dn.rearrange("p (h v) -> p h v", v=1).to_broadcast([P, 4, DV])
                        dst = Hs[:, c - 2, 4 * hh:4 * hh + 4, :]
                        if (d, c) in ((0, 2), (1, 3)):
                            TT(dst, t1[:, :, 0:DV], db, ALU.mult).then_inc(num_done, 1)
                        else:
                            link(TT(t1[:, :, 0:DV], t1[:, :, 0:DV], db, ALU.mult))
                            TT(dst, dst, t1[:, :, 0:DV], ALU.add).then_inc(num_done, 1)
                if i in (26, 28, 30, 32):
                    p = (i - 26) // 2
                    bk = bank_of(f"lg{p}")
                    dve.wait_ge(lo_copy, 2 + p + 1)
                    TT(lgs[:, 2 * p:2 * p + 2, :], ps[:, bk:bk + 2, 0:256], lgs[:, 2 * p:2 * p + 2, :], ALU.add).then_inc(
                        bulk_free[BULK.index(f"lg{p}") % 2], 1)
                if i == 35:
                    dve.wait_ge(gelu_done, 1)
                    v = lgs.rearrange("p b (c r) -> p b c r", r=ROWS)
                    TT(v, v, LO.rearrange("p b (r c) -> p b c r", r=ROWS), ALU.mult).then_inc(lru_mul, 1)
                if i == 37:
                    dve.wait_ge(mxa_hi, 1)
                    TT(MXA[:, 1], lgs, MXA[:, 0].bitcast(F), ALU.subtract).then_inc(mxa_done, 1)
                if i in (40, 44):
                    c = 1 if i == 40 else 0
                    q = lgs.rearrange("p b t -> p (b t)")[:, 0:1024].rearrange("p (h v) -> p h v", h=8)
                    dve.wait_ge(mxa_done, 1)
                    dve.wait_ge(num_done, 6 if c else 8)
                    link(TT(q, Hs[:, c], Hs[:, c], ALU.mult))
                    nc.vector.reduce_sum(mst[:, 48 + 8 * c:56 + 8 * c], q, AX.X).then_inc(hms, 1)
                if i in (41, 45):
                    c = 1 if i == 41 else 0
                    dve.wait_ge(hroot, 1 + (i == 45))
                    r = mst[:, 48 + 8 * c:56 + 8 * c]
                    link(nc.vector.reciprocal(r, r))
                    link(TT(Hs[:, c], Hs[:, c], r.rearrange("p (h v) -> p h v", v=1).to_broadcast([P, 8, DV]), ALU.mult))
                    for q in ("o0", "o1"):
                        dve.wait_ge(bulk_free[BULK.index(q) % 2], BULK.index(q) // 2 + 1)
                    TT(Hs[:, c], Hs[:, c], SO[:, c].rearrange("p (h v) -> p h v", h=8), ALU.mult).then_inc(hn_done, 1)
                if i == 47:
                    extra_ready("ht")
                    m32 = Hs.rearrange("p c h v -> p (c h v)").rearrange("p (h c t) -> p h c t", h=8, c=2)
                    for c in range(2):
                        last = TT(m32[:, :, c, :], ps[:, 4 + 2 * c:6 + 2 * c, :].rearrange("p b (h t) -> p (b h) t", h=4),
                                  v_("mnorm").rearrange("p (h t) -> p h t", t=1).to_broadcast([P, 8, P]), ALU.mult)
                    last.then_inc(ext_free, 1)
                if i == 48:
                    dve.wait_ge(mxb_hi, 1)
                    TT(MXB[:, 1], Hs.rearrange("p c h v -> p (c h v)").rearrange("p (h t) -> p h t", h=8),
                       MXB[:, 0].bitcast(F), ALU.subtract).then_inc(mxb_done, 1)
                if i >= 41:
                    kind, p, _ = MIX_UNITS[i]
                    name = f"{kind}{p}"
                    bk = bank_of(name)
                    unit_done(dve, kind, p, 0)
                    for part in range(2):
                        for ct in range(2):
                            d = 2 * p + ct
                            last = STT(X[:, 1, d, :], ps[:, bk + ct, part * 256:(part + 1) * 256],
                                       modx[:, 5, d:d + 1], X[:, 1, d, :], ALU.mult, ALU.add)
                        if part == 0:
                            link(last)
                    last.then_inc(bulk_free[BULK.index(name) % 2], 1)

            for i in range(len(MIX_UNITS)):
                if i >= 1:
                    split(MIX + i + 1)
                if i >= 50:
                    add_squares(2, 2 * (i - 50), 2 * (i - 49), SEQ)
                tick(i)

            add_squares(2, 14, DT, SEQ)
            split(FF2 + 1)
            inverse(2, SEQ)
            norm_tiles(2, True)
            dve.wait_ge(sum_zero, 1)
            with nc.vector.Fori(0, GROUPS - 1) as g:
                ffn(FF2, H_FF2, 1, g, True)
            ffn(FF2, H_FF2, 1, GROUPS - 1, True, last_group=True, norm=3)
            add_squares(3, 12, DT, SEQ)

            inverse(3, SEQ)
            for d in range(DT):
                ins = STT(X[:, 0, d, :], X[:, 1, d, :], v_("nf", d, d + 1), rms[:, 0:SEQ], ALU.mult, ALU.mult)
                if d % 4 == 3:
                    ins.then_inc(out_ready, 1)


_NAMES = ["xT", "vec", "cst", "lru_w", "ada_w", "w_up1", "w_dn1", "w_in", "w_out", "w_up2", "w_dn2"]


def constants():
    import numpy as np

    k = np.zeros((P, NCST), np.float32)

    def put(name, rows, value):
        lo, hi = CST[name]
        k[0:rows, lo:hi] = value

    t = np.arange(P)
    put("ident", P, np.eye(P))
    put("maskf", P, np.where(t[:, None] <= t[None, :], 0.0, -1e30))
    put("maskb", P, np.where(t[:, None] >= t[None, :], 0.0, -1e30))
    put("ones", P, 1.0)
    put("one", P, 1.0)
    put("eps", P, EPS)
    r = np.arange(40)
    live = (r < 8) | (r >= 32)
    put("parity", 40, (live[:, None] & ((r[:, None] % 2) == (t[None, :] >= 64))))
    jj = np.zeros((40, 2, 4, 4))
    sel = np.zeros((32, 2, 40))
    for h in range(HEADS):
        for d in range(2):
            jj[32 * d + h, d, :, h // 2] = 1
            sel[16 * d + h, 0, 32 * d + h] = 1
            sel[16 * d + 8 + h, 1, 32 * d + h] = 1
    put("jj", 40, jj.reshape(40, 32))
    put("sel", 32, sel.reshape(32, 80))
    put("comb", 4, np.array([[1, 0], [1, 0], [0, 1], [0, 1]]))
    return k


def kernel(**inp):
    import numpy as np
    import concourse.bacc as bacc
    from concourse import mybir as mb
    from concourse.bass_utils import run_bass_kernel_spmd

    a = {k: np.asarray(v) for k, v in inp.items()}

    def cols(v):
        return np.ascontiguousarray(v.reshape(-1, P).T)

    lat = a["x"][0].reshape(ROWS, GRID_W, D_MODEL).transpose(1, 0, 2).reshape(SEQ, D_MODEL)
    xT = np.concatenate([v.T.reshape(DT, P, SEQ).transpose(1, 0, 2) for v in (a["ctx"][0], lat)], axis=1)
    mg = np.zeros((P, 2), a["b_mgate"].dtype)
    gates = a["b_mgate"][0].reshape(2, 2, HEADS)
    for d in range(2):
        for q in range(2):
            mg[32 * d:32 * d + HEADS, q] = gates[d, q]
    ada_b = cols(a["ada_b"][0])
    vec = np.concatenate([
        ada_b, ada_b[:, 0:DT], *(ada_b[:, b * DT:(b + 1) * DT] for _, b in LATE),
        cols(a["ffn1_norm"][0]), cols(a["mix_norm"][0]), cols(a["ffn2_norm"][0]),
        cols(a["final_norm"]), cols(a["lru_conv_w"][0].reshape(-1)), cols(a["lru_conv_b"][0]),
        cols(a["lru_b_r"][0].reshape(-1)), cols(a["lru_b_i"][0].reshape(-1)), cols(a["lru_lam"][0].reshape(-1)),
        cols(a["c_ctx"]), cols(a["c"][0]), mg, cols(a["mlstm_norm"][0])], axis=1)
    lru_w = np.stack([a["lru_w_r"][0, 0], a["lru_w_i"][0, 0], a["lru_w_r"][0, 1], a["lru_w_i"][0, 1]]).transpose(2, 1, 0, 3)
    arrays = {"xT": xT, "vec": vec, "cst": constants(), "lru_w": lru_w, "ada_w": a["ada_w"][0],
              "w_up1": a["ffn1_w_up"][0], "w_dn1": a["ffn1_w_down"][0], "w_in": a["w_in"][0], "w_out": a["w_out"][0],
              "w_up2": a["ffn2_w_up"][0], "w_dn2": a["ffn2_w_down"][0]}
    arrays = {k: np.ascontiguousarray(v) for k, v in arrays.items()}
    nc = bacc.Bacc("TRN2", target_bir_lowering=False, num_devices=1, dynamic_dma_scratch_size=1024)
    aps = [nc.dram_tensor(f"in_{k}", arrays[k].shape, mb.dt.from_np(arrays[k].dtype), kind="ExternalInput").ap()
           for k in _NAMES]
    out = nc.dram_tensor("out_y", (P, DT, SEQ), mb.dt.float32, kind="ExternalOutput").ap()
    hybrid_layer(nc, *aps, out)
    r = run_bass_kernel_spmd(nc, [{f"in_{k}": arrays[k] for k in _NAMES}], core_ids=[0])
    y = r.results[0]["out_y"]
    y = y.transpose(2, 1, 0).reshape(GRID_W, ROWS, D_MODEL).transpose(1, 0, 2).reshape(1, SEQ, D_MODEL)
    return np.ascontiguousarray(y)
```
